# Optimizing a Trainium2 kernel written in Bass

```python
import math
import jax, jax.numpy as jnp
from jax import lax
import numpy as np

D_MODEL = 1024
BATCH = 1
SEQ = 256
DEPTH = 2

N_MIXERS = 4
D_FF = 2816
MEM_LEN = 256
X_HEADS = 4
X_HEAD_DIM = 128
X_WIDTH = X_HEADS * X_HEAD_DIM
POOL_WINDOWS = (2, 4, 8, 16)
POOL_GROUPS = len(POOL_WINDOWS)
POOL_GROUP_DIM = D_MODEL // POOL_GROUPS
DIFF_HEAD_DIM = 64
DIFF_HEADS = D_MODEL // (2 * DIFF_HEAD_DIM)
DIFF_QK = DIFF_HEADS * 2 * DIFF_HEAD_DIM
DIFF_V = DIFF_HEADS * 2 * DIFF_HEAD_DIM
Q_BLOCK = 128
MLSTM_HEADS = 4
MLSTM_HEAD_DIM = D_MODEL // MLSTM_HEADS
MLSTM_CONV = 4
MLSTM_CHUNK = 64
GLA_HEADS = 4
GLA_KEY_DIM = D_MODEL // 2 // GLA_HEADS
GLA_VALUE_DIM = D_MODEL // GLA_HEADS
GLA_GATE_RANK = 16
GLA_TAU = 16.0
GLA_CHUNK = 64
NORM_EPS = 1e-6
SUBLN_EPS = 1e-5
POOL_IN = D_MODEL + X_WIDTH
DIFF_IN = 2 * DIFF_QK + DIFF_V + X_WIDTH
MLSTM_IN = 4 * D_MODEL + 2 * MLSTM_HEADS + X_WIDTH
GLA_IN = 2 * GLA_HEADS * GLA_KEY_DIM + 2 * D_MODEL + GLA_GATE_RANK + X_WIDTH
MIX_OUT = D_MODEL + X_WIDTH


def rmsnorm(x, g, eps=NORM_EPS):
    x32 = x.astype(jnp.float32)
    y = x32 * lax.rsqrt(jnp.mean(x32 * x32, axis=-1, keepdims=True) + eps)
    return (y * g.astype(jnp.float32)).astype(x.dtype)

def swiglu(h, w_up, w_down):
    gate, up = jnp.split(h @ w_up, 2, axis=-1)
    return (jax.nn.silu(gate) * up) @ w_down

def causal_conv(x, w):
    K, C = w.shape
    return lax.conv_general_dilated(x, w[:, None, :].astype(x.dtype), (1,), [(K - 1, 0)],
                                    dimension_numbers=('NWC', 'WIO', 'NWC'), feature_group_count=C)

def alibi_slopes(n):
    return jnp.asarray([2.0 ** (-8.0 * (h + 1) / n) for h in range(n)], dtype=jnp.float32)

def memory_attention(xq, mem_k, mem_v):
    B, S, _ = xq.shape
    q = xq.reshape(B, S, X_HEADS, X_HEAD_DIM)
    s = jnp.einsum('bshd,bmhd->bhsm', q, mem_k).astype(jnp.float32) * (X_HEAD_DIM ** -0.5)
    p = jax.nn.softmax(s, axis=-1)
    o = jnp.einsum('bhsm,bmhd->bshd', p.astype(mem_v.dtype), mem_v)
    return o.reshape(B, S, X_WIDTH)

def _chunks(a, L):
    B, H, S = a.shape[:3]
    return jnp.moveaxis(a.reshape(B, H, S // L, L, *a.shape[3:]), 2, 0)

def _unchunk(a):
    NC, B, H, L = a.shape[:4]
    return jnp.moveaxis(a, 0, 2).reshape(B, H, NC * L, *a.shape[4:])

def multiscale_pool(u, w_group, scale):
    B, S, _ = u.shape
    u32 = u.astype(jnp.float32).reshape(B, S, POOL_GROUPS, POOL_GROUP_DIM)
    cs = jnp.cumsum(u32, axis=1)
    outs = []
    for g, w in enumerate(POOL_WINDOWS):
        c = cs[:, :, g]
        prev = jnp.pad(c[:, :S - w], ((0, 0), (w, 0), (0, 0)))
        count = jnp.minimum(jnp.arange(1, S + 1), w).astype(jnp.float32)
        outs.append((c - prev) / count[None, :, None] - u32[:, :, g])
    pooled = jnp.stack(outs, axis=2).astype(u.dtype)
    mixed = jnp.einsum('bsgc,gcd->bsgd', pooled, w_group).reshape(B, S, D_MODEL)
    return mixed * scale

def pool_layer(h, w_in, w_group, scale, w_out, mem_k, mem_v):
    proj = h @ w_in
    u, xq = proj[..., :D_MODEL], proj[..., D_MODEL:]
    mix = multiscale_pool(u, w_group, scale)
    xo = memory_attention(xq, mem_k, mem_v)
    return jnp.concatenate([mix, xo], axis=-1) @ w_out

def diff_attention(q, k, v, lam, slopes):
    S = q.shape[3]
    scale = DIFF_HEAD_DIM ** -0.5
    outs = []
    for start in range(0, S, Q_BLOCK):
        end = start + Q_BLOCK
        dist = (jnp.arange(start, end)[:, None] - jnp.arange(end)[None, :]).astype(jnp.float32)
        bias = jnp.where(dist >= 0, -slopes[:, None, None] * dist, -jnp.inf)
        s = jnp.einsum('bhcqd,bhckd->bhcqk', q[:, :, :, start:end], k[:, :, :, :end]).astype(jnp.float32) * scale
        p = jax.nn.softmax(s + bias[None, :, None], axis=-1)
        w = p[:, :, 0] - lam * p[:, :, 1]
        outs.append(jnp.einsum('bhqk,bhkd->bhqd', w.astype(v.dtype), v[:, :, :end]))
    return jnp.concatenate(outs, axis=2)

def diff_layer(h, w_in, lam_p, norm_g, w_out, mem_k, mem_v, slopes, layer_idx):
    B, S, _ = h.shape
    H, Dh = DIFF_HEADS, DIFF_HEAD_DIM
    proj = h @ w_in
    q = proj[..., :DIFF_QK].reshape(B, S, H, 2, Dh).transpose(0, 2, 3, 1, 4)
    k = proj[..., DIFF_QK:2 * DIFF_QK].reshape(B, S, H, 2, Dh).transpose(0, 2, 3, 1, 4)
    v = proj[..., 2 * DIFF_QK:2 * DIFF_QK + DIFF_V].reshape(B, S, H, 2 * Dh).transpose(0, 2, 1, 3)
    xq = proj[..., 2 * DIFF_QK + DIFF_V:]
    lam_init = 0.8 - 0.6 * math.exp(-0.3 * layer_idx)
    lp = lam_p.astype(jnp.float32)
    lam = jnp.exp(jnp.sum(lp[0] * lp[1])) - jnp.exp(jnp.sum(lp[2] * lp[3])) + lam_init
    o = diff_attention(q, k, v, lam, slopes)
    o = rmsnorm(o, norm_g, eps=SUBLN_EPS) * (1.0 - lam_init)
    o = o.transpose(0, 2, 1, 3).reshape(B, S, H * 2 * Dh)
    xo = memory_attention(xq, mem_k, mem_v)
    return jnp.concatenate([o, xo], axis=-1) @ w_out

def mlstm_chunkwise(q, k, v, i_pre, f_pre):
    B, H, S, Dk = q.shape
    Dv = v.shape[-1]
    L = MLSTM_CHUNK
    q = q * (Dk ** -0.5)
    lf = jax.nn.log_sigmoid(f_pre)
    causal = jnp.tril(jnp.ones((L, L), dtype=bool))

    def step(carry, inp):
        C, n, m = carry
        qc, kc, vc, ic, lfc = inp
        b = jnp.cumsum(lfc, axis=-1)
        dmat = jnp.where(causal, b[..., :, None] - b[..., None, :] + ic[..., None, :], -jnp.inf)
        inter = b + m[..., None]
        m_t = jnp.maximum(inter, jnp.max(dmat, axis=-1))
        dec = jnp.exp(inter - m_t)
        sqk = jnp.einsum('bhtd,bhsd->bhts', qc, kc) * jnp.exp(dmat - m_t[..., None])
        num = dec[..., None] * jnp.einsum('bhtd,bhde->bhte', qc, C) + jnp.einsum('bhts,bhse->bhte', sqk, vc)
        den = dec * jnp.einsum('bhtd,bhd->bht', qc, n) + jnp.sum(sqk, axis=-1)
        hc = num / jnp.maximum(jnp.abs(den), jnp.exp(-m_t))[..., None]
        bL = b[..., -1]
        gs = bL[..., None] - b + ic
        m_new = jnp.maximum(bL + m, jnp.max(gs, axis=-1))
        ws = jnp.exp(gs - m_new[..., None])
        carry_dec = jnp.exp(bL + m - m_new)
        C_new = carry_dec[..., None, None] * C + jnp.einsum('bhs,bhsd,bhse->bhde', ws, kc, vc)
        n_new = carry_dec[..., None] * n + jnp.einsum('bhs,bhsd->bhd', ws, kc)
        return (C_new, n_new, m_new), hc

    init = (jnp.zeros((B, H, Dk, Dv), jnp.float32), jnp.zeros((B, H, Dk), jnp.float32),
            jnp.zeros((B, H), jnp.float32))
    xs = (_chunks(q, L), _chunks(k, L), _chunks(v, L), _chunks(i_pre, L), _chunks(lf, L))
    _, hs = lax.scan(step, init, xs)
    return _unchunk(hs)

def mlstm_layer(h, w_in, conv_w, gate_b, norm_g, w_out, mem_k, mem_v):
    B, S, _ = h.shape
    H, Dh, D = MLSTM_HEADS, MLSTM_HEAD_DIM, D_MODEL
    proj = h @ w_in
    qk = jax.nn.silu(causal_conv(proj[..., :2 * D], conv_w))
    q, k = qk[..., :D], qk[..., D:]
    v = proj[..., 2 * D:3 * D]
    o = proj[..., 3 * D:4 * D]
    gates = proj[..., 4 * D:4 * D + 2 * H].astype(jnp.float32).reshape(B, S, 2, H) + gate_b.astype(jnp.float32)
    xq = proj[..., 4 * D + 2 * H:]

    def heads(a):
        return a.reshape(B, S, H, Dh).transpose(0, 2, 1, 3).astype(jnp.float32)

    hh = mlstm_chunkwise(heads(q), heads(k), heads(v),
                         gates[:, :, 0].transpose(0, 2, 1), gates[:, :, 1].transpose(0, 2, 1))
    hh = rmsnorm(hh.transpose(0, 2, 1, 3).astype(h.dtype), norm_g.reshape(H, Dh)).reshape(B, S, D)
    hh = hh * jax.nn.sigmoid(o)
    xo = memory_attention(xq, mem_k, mem_v)
    return jnp.concatenate([hh, xo], axis=-1) @ w_out

def gla_chunkwise(q, k, v, log_a):
    B, H, S, Dk = q.shape
    Dv = v.shape[-1]
    L = GLA_CHUNK
    q = q * (Dk ** -0.5)
    causal = jnp.tril(jnp.ones((L, L), dtype=bool))

    def step(state, inp):
        qc, kc, vc, ac = inp
        b = jnp.cumsum(ac, axis=2)
        inter = jnp.einsum('bhtd,bhde->bhte', qc * jnp.exp(b), state)
        diff = b[:, :, :, None, :] - b[:, :, None, :, :]
        decay = jnp.exp(jnp.where(causal[:, :, None], diff, -jnp.inf))
        amat = jnp.einsum('bhtd,bhsd,bhtsd->bhts', qc, kc, decay)
        intra = jnp.einsum('bhts,bhse->bhte', amat, vc)
        bL = b[:, :, -1]
        k_dec = kc * jnp.exp(bL[:, :, None, :] - b)
        new_state = jnp.exp(bL)[..., None] * state + jnp.einsum('bhsd,bhse->bhde', k_dec, vc)
        return new_state, inter + intra

    init = jnp.zeros((B, H, Dk, Dv), jnp.float32)
    xs = (_chunks(q, L), _chunks(k, L), _chunks(v, L), _chunks(log_a, L))
    _, os_ = lax.scan(step, init, xs)
    return _unchunk(os_)

def gla_layer(h, w_in, gate_w2, gate_b, norm_g, w_out, mem_k, mem_v):
    B, S, _ = h.shape
    H, Dk, Dv = GLA_HEADS, GLA_KEY_DIM, GLA_VALUE_DIM
    kw = H * Dk
    proj = h @ w_in
    q = proj[..., :kw]
    k = proj[..., kw:2 * kw]
    v = proj[..., 2 * kw:2 * kw + D_MODEL]
    g = proj[..., 2 * kw + D_MODEL:2 * kw + 2 * D_MODEL]
    z = proj[..., 2 * kw + 2 * D_MODEL:2 * kw + 2 * D_MODEL + GLA_GATE_RANK]
    xq = proj[..., 2 * kw + 2 * D_MODEL + GLA_GATE_RANK:]
    log_a = jax.nn.log_sigmoid((z @ gate_w2 + gate_b).astype(jnp.float32)) / GLA_TAU

    def heads(a, d):
        return a.reshape(B, S, H, d).transpose(0, 2, 1, 3).astype(jnp.float32)

    o = gla_chunkwise(heads(q, Dk), heads(k, Dk), heads(v, Dv), heads(log_a, Dk))
    o = rmsnorm(o.transpose(0, 2, 1, 3).astype(h.dtype), norm_g.reshape(H, Dv)).reshape(B, S, D_MODEL)
    o = o * jax.nn.silu(g)
    xo = memory_attention(xq, mem_k, mem_v)
    return jnp.concatenate([o, xo], axis=-1) @ w_out

def _layers_of(kind):
    return len(range(kind, DEPTH, N_MIXERS))

def first_inputs(seed: int = 0) -> dict:
    key = jax.random.key(seed)
    keys = iter(jax.random.split(key, 40))

    def nrm(shape, scale):
        return jax.random.normal(next(keys), shape, jnp.float32) * scale

    def gain(shape):
        return 1.0 + nrm(shape, 0.05)

    nA, nB, nC, nD = (_layers_of(kd) for kd in range(N_MIXERS))
    D = D_MODEL
    x = nrm((BATCH, SEQ, D), 1.0)
    mem = nrm((BATCH, MEM_LEN, D), 1.0)
    norm_g = gain((DEPTH, 3, D))
    ffn_w_up = nrm((DEPTH, 2, D, 2 * D_FF), D ** -0.5)
    ffn_w_down = nrm((DEPTH, 2, D_FF, D), D_FF ** -0.5)
    mem_norm_g = gain((D,))
    mem_w_kv = nrm((DEPTH, D, 2 * X_WIDTH), D ** -0.5)
    pool_w_in = nrm((nA, D, POOL_IN), D ** -0.5)
    pool_w_group = nrm((nA, POOL_GROUPS, POOL_GROUP_DIM, POOL_GROUP_DIM), POOL_GROUP_DIM ** -0.5)
    pool_scale = gain((nA, D))
    pool_w_out = nrm((nA, MIX_OUT, D), MIX_OUT ** -0.5)
    diff_w_in = nrm((nB, D, DIFF_IN), D ** -0.5)
    diff_lambda = nrm((nB, 4, DIFF_HEAD_DIM), 0.1)
    diff_norm_g = gain((nB, 2 * DIFF_HEAD_DIM))
    diff_w_out = nrm((nB, MIX_OUT, D), MIX_OUT ** -0.5)
    mlstm_w_in = nrm((nC, D, MLSTM_IN), D ** -0.5)
    mlstm_conv_w = nrm((nC, MLSTM_CONV, 2 * D), MLSTM_CONV ** -0.5)
    i_bias = nrm((nC, MLSTM_HEADS), 0.1)
    f_bias = jnp.linspace(3.0, 6.0, MLSTM_HEADS, dtype=jnp.float32)[None] + nrm((nC, MLSTM_HEADS), 0.01)
    mlstm_gate_b = jnp.stack([i_bias, f_bias], axis=1)
    mlstm_norm_g = gain((nC, D))
    mlstm_w_out = nrm((nC, MIX_OUT, D), MIX_OUT ** -0.5)
    gla_w_in = nrm((nD, D, GLA_IN), D ** -0.5)
    gla_gate_w2 = nrm((nD, GLA_GATE_RANK, GLA_HEADS * GLA_KEY_DIM), GLA_GATE_RANK ** -0.5)
    gla_gate_b = nrm((nD, GLA_HEADS * GLA_KEY_DIM), 0.1)
    gla_norm_g = gain((nD, D))
    gla_w_out = nrm((nD, MIX_OUT, D), MIX_OUT ** -0.5)
    final_norm_g = gain((D,))
    return {'x': x, 'mem': mem, 'norm_g': norm_g, 'ffn_w_up': ffn_w_up, 'ffn_w_down': ffn_w_down,
            'mem_norm_g': mem_norm_g, 'mem_w_kv': mem_w_kv,
            'pool_w_in': pool_w_in, 'pool_w_group': pool_w_group, 'pool_scale': pool_scale, 'pool_w_out': pool_w_out,
            'diff_w_in': diff_w_in, 'diff_lambda': diff_lambda, 'diff_norm_g': diff_norm_g, 'diff_w_out': diff_w_out,
            'mlstm_w_in': mlstm_w_in, 'mlstm_conv_w': mlstm_conv_w, 'mlstm_gate_b': mlstm_gate_b,
            'mlstm_norm_g': mlstm_norm_g, 'mlstm_w_out': mlstm_w_out,
            'gla_w_in': gla_w_in, 'gla_gate_w2': gla_gate_w2, 'gla_gate_b': gla_gate_b,
            'gla_norm_g': gla_norm_g, 'gla_w_out': gla_w_out, 'final_norm_g': final_norm_g}

def first_block(x, mem, norm_g, ffn_w_up, ffn_w_down, mem_norm_g, mem_w_kv,
              pool_w_in, pool_w_group, pool_scale, pool_w_out,
              diff_w_in, diff_lambda, diff_norm_g, diff_w_out,
              mlstm_w_in, mlstm_conv_w, mlstm_gate_b, mlstm_norm_g, mlstm_w_out,
              gla_w_in, gla_gate_w2, gla_gate_b, gla_norm_g, gla_w_out, final_norm_g):
    B, M, _ = mem.shape
    mem_n = rmsnorm(mem, mem_norm_g)
    slopes = alibi_slopes(DIFF_HEADS)
    for i in range(DEPTH):
        kind, j = i % N_MIXERS, i // N_MIXERS
        kv = mem_n @ mem_w_kv[i]
        mem_k = kv[..., :X_WIDTH].reshape(B, M, X_HEADS, X_HEAD_DIM)
        mem_v = kv[..., X_WIDTH:].reshape(B, M, X_HEADS, X_HEAD_DIM)
        x = x + 0.5 * swiglu(rmsnorm(x, norm_g[i, 0]), ffn_w_up[i, 0], ffn_w_down[i, 0])
        h = rmsnorm(x, norm_g[i, 1])
        if kind == 0:
            mix = pool_layer(h, pool_w_in[j], pool_w_group[j], pool_scale[j], pool_w_out[j], mem_k, mem_v)
        elif kind == 1:
            mix = diff_layer(h, diff_w_in[j], diff_lambda[j], diff_norm_g[j], diff_w_out[j], mem_k, mem_v, slopes, i)
        elif kind == 2:
            mix = mlstm_layer(h, mlstm_w_in[j], mlstm_conv_w[j], mlstm_gate_b[j], mlstm_norm_g[j], mlstm_w_out[j],
                              mem_k, mem_v)
        else:
            mix = gla_layer(h, gla_w_in[j], gla_gate_w2[j], gla_gate_b[j], gla_norm_g[j], gla_w_out[j], mem_k, mem_v)
        x = x + mix
        x = x + 0.5 * swiglu(rmsnorm(x, norm_g[i, 2]), ffn_w_up[i, 1], ffn_w_down[i, 1])
    return rmsnorm(x, final_norm_g)


DEPTH_2 = 1

N_MEM = 256
NEG_INF = -1e30

MIX_WIDTH = D_MODEL
MOBA_WIDTH = MIX_WIDTH // 2
RET_WIDTH = MIX_WIDTH - MOBA_WIDTH

MOBA_HEAD_DIM = 64
MOBA_HEADS = MOBA_WIDTH // MOBA_HEAD_DIM
MOBA_BLOCK = 256
MOBA_TOPK = 3
MOBA_Q_BLOCK = 32
ROPE_THETA = 500000.0
ROPE_DIM = MOBA_HEAD_DIM // 4

RET_HEADS = 4
RET_V_DIM = RET_WIDTH // RET_HEADS
RET_QK_DIM = RET_V_DIM // 2
RET_CHUNK = 128
RET_THETA = 10000.0

CROSS_HEADS = 4
CROSS_HEAD_DIM = D_MODEL // CROSS_HEADS

D_FF_2 = -(-8 * D_MODEL // (3 * 256)) * 256

W_MQ = MOBA_WIDTH
W_MK = MOBA_WIDTH
W_MV = MOBA_WIDTH
W_RQ = RET_HEADS * RET_QK_DIM
W_RK = RET_HEADS * RET_QK_DIM
W_RV = RET_WIDTH
W_RG = RET_WIDTH
IN_PROJ_WIDTH = W_MQ + W_MK + W_MV + W_RQ + W_RK + W_RV + W_RG
SPLIT_POINTS = [W_MQ, W_MQ + W_MK, W_MQ + W_MK + W_MV,
                W_MQ + W_MK + W_MV + W_RQ,
                W_MQ + W_MK + W_MV + W_RQ + W_RK,
                W_MQ + W_MK + W_MV + W_RQ + W_RK + W_RV]


def rms_norm(x, g):
    xf = x.astype(jnp.float32)
    y = xf * lax.rsqrt(jnp.mean(xf * xf, axis=-1, keepdims=True) + NORM_EPS)
    return (y * g.astype(jnp.float32)).astype(x.dtype)

def rotary(x, inv_freq, rot_dim):
    S = x.shape[2]
    half = rot_dim // 2
    ang = jnp.arange(S, dtype=jnp.float32)[:, None] * inv_freq[None, :]
    cos, sin = jnp.cos(ang), jnp.sin(ang)
    xr = x[..., :rot_dim].astype(jnp.float32)
    x1, x2 = xr[..., :half], xr[..., half:]
    rot = jnp.concatenate([x1 * cos - x2 * sin, x2 * cos + x1 * sin], axis=-1).astype(x.dtype)
    return jnp.concatenate([rot, x[..., rot_dim:]], axis=-1)

def split_heads(t, n_heads):
    B, S, _ = t.shape
    return t.reshape(B, S, n_heads, -1).transpose(0, 2, 1, 3)

def merge_heads(t):
    B, H, S, d = t.shape
    return t.transpose(0, 2, 1, 3).reshape(B, S, H * d)

def moba_attention(q, k, v):
    B, H, S, dh = q.shape
    L = MOBA_BLOCK
    nb = -(-S // L)
    pad = nb * L - S
    kp = jnp.pad(k, ((0, 0), (0, 0), (0, pad), (0, 0)))
    vp = jnp.pad(v, ((0, 0), (0, 0), (0, pad), (0, 0)))
    k_blocks = kp.reshape(B, H, nb, L, dh)
    v_blocks = vp.reshape(B, H, nb, L, dh)
    k_mean = jnp.mean(k_blocks.astype(jnp.float32), axis=3).astype(q.dtype)
    n_sel = min(MOBA_TOPK, nb)
    scale = dh ** -0.5
    QB = MOBA_Q_BLOCK
    nq = S // QB
    q_blocks = q.reshape(B, H, nq, QB, dh).transpose(2, 0, 1, 3, 4)
    b_idx = jnp.arange(B)[:, None, None, None]
    h_idx = jnp.arange(H)[None, :, None, None]
    block_ids = jnp.arange(nb)
    slot_ids = jnp.arange(n_sel)
    key_offsets = jnp.arange(L)

    def one_query_block(args):
        qb, qi = args
        q_pos = qi * QB + jnp.arange(QB)
        cur = (qi * QB) // L
        gate = jnp.einsum('bhqd,bhnd->bhqn', qb, k_mean).astype(jnp.float32)
        gate = jnp.where((block_ids < cur)[None, None, None, :], gate, NEG_INF)
        _, sel = lax.top_k(gate, n_sel)
        slot_valid = slot_ids < cur
        k_sel = k_blocks[b_idx, h_idx, sel]
        v_sel = v_blocks[b_idx, h_idx, sel]
        s_sel = jnp.einsum('bhqd,bhqnld->bhqnl', qb, k_sel).astype(jnp.float32) * scale
        s_sel = jnp.where(slot_valid[:, None], s_sel, NEG_INF)
        k_own = lax.dynamic_index_in_dim(k_blocks, cur, axis=2, keepdims=False)
        v_own = lax.dynamic_index_in_dim(v_blocks, cur, axis=2, keepdims=False)
        s_own = jnp.einsum('bhqd,bhld->bhql', qb, k_own).astype(jnp.float32) * scale
        own_pos = cur * L + key_offsets
        s_own = jnp.where(own_pos[None, :] <= q_pos[:, None], s_own, NEG_INF)
        logits = jnp.concatenate([s_sel.reshape(B, H, QB, n_sel * L), s_own], axis=-1)
        p = jax.nn.softmax(logits, axis=-1)
        p_sel = p[..., :n_sel * L].reshape(B, H, QB, n_sel, L).astype(v.dtype)
        p_own = p[..., n_sel * L:].astype(v.dtype)
        return (jnp.einsum('bhqnl,bhqnld->bhqd', p_sel, v_sel)
                + jnp.einsum('bhql,bhld->bhqd', p_own, v_own))

    out = lax.map(one_query_block, (q_blocks, jnp.arange(nq)))
    return out.transpose(1, 2, 0, 3, 4).reshape(B, H, S, dh)

def retention(q, k, v):
    B, H, S, dk = q.shape
    dv = v.shape[-1]
    C = RET_CHUNK
    nc = S // C
    log_g = jnp.log(1.0 - jnp.power(2.0, -5.0 - jnp.arange(H, dtype=jnp.float32)))
    idx = jnp.arange(C, dtype=jnp.float32)
    diff = idx[:, None] - idx[None, :]
    inner_decay = jnp.where(diff >= 0, jnp.exp(log_g[:, None, None] * jnp.maximum(diff, 0.0)), 0.0)
    q_decay = jnp.exp(log_g[:, None] * (idx + 1.0))[None, :, :, None]
    k_decay = jnp.exp(log_g[:, None] * (C - 1.0 - idx))[None, :, :, None]
    chunk_decay = jnp.exp(log_g * C)[None, :, None, None]

    def to_chunks(t):
        return t.astype(jnp.float32).reshape(B, H, nc, C, t.shape[-1]).transpose(2, 0, 1, 3, 4)

    def step(state, inp):
        qc, kc, vc = inp
        attn = jnp.einsum('bhid,bhjd->bhij', qc, kc) * inner_decay[None]
        inner = jnp.einsum('bhij,bhjv->bhiv', attn, vc)
        cross = jnp.einsum('bhid,bhdv->bhiv', qc * q_decay, state)
        new_state = state * chunk_decay + jnp.einsum('bhjd,bhjv->bhdv', kc * k_decay, vc)
        return new_state, inner + cross

    state0 = jnp.zeros((B, H, dk, dv), jnp.float32)
    _, out = lax.scan(step, state0, (to_chunks(q), to_chunks(k), to_chunks(v)))
    return out.transpose(1, 2, 0, 3, 4).reshape(B, H, S, dv)

def cross_attention(h, mem_n, w_cq, w_ckv, w_co):
    q = split_heads(h @ w_cq, CROSS_HEADS)
    kv = mem_n @ w_ckv
    k = split_heads(kv[..., :D_MODEL], CROSS_HEADS)
    v = split_heads(kv[..., D_MODEL:], CROSS_HEADS)
    s = jnp.einsum('bhsd,bhmd->bhsm', q, k).astype(jnp.float32) * (CROSS_HEAD_DIM ** -0.5)
    p = jax.nn.softmax(s, axis=-1).astype(v.dtype)
    o = jnp.einsum('bhsm,bhmd->bhsd', p, v)
    return merge_heads(o) @ w_co

def second_inputs(seed: int = 0) -> dict:
    key = jax.random.key(seed)
    ks = jax.random.split(key, 16)

    def w(k, shape, fan_in):
        return jax.random.normal(k, shape, jnp.float32) * (fan_in ** -0.5)

    def gain(k):
        return 1.0 + 0.05 * jax.random.normal(k, (DEPTH_2, D_MODEL), jnp.float32)

    return {
        "x": jax.random.normal(ks[0], (BATCH, SEQ, D_MODEL), jnp.float32),
        "mem": jax.random.normal(ks[1], (BATCH, N_MEM, D_MODEL), jnp.float32),
        "g_pre_mix": gain(ks[2]),
        "w_in": w(ks[3], (DEPTH_2, D_MODEL, IN_PROJ_WIDTH), D_MODEL),
        "w_out": w(ks[4], (DEPTH_2, MIX_WIDTH, D_MODEL), MIX_WIDTH),
        "g_post_mix": gain(ks[5]),
        "g_pre_cross": gain(ks[6]),
        "g_mem": gain(ks[7]),
        "w_cq": w(ks[8], (DEPTH_2, D_MODEL, D_MODEL), D_MODEL),
        "w_ckv": w(ks[9], (DEPTH_2, D_MODEL, 2 * D_MODEL), D_MODEL),
        "w_co": w(ks[10], (DEPTH_2, D_MODEL, D_MODEL), D_MODEL),
        "g_post_cross": gain(ks[11]),
        "g_pre_ffn": gain(ks[12]),
        "w_gate_up": w(ks[13], (DEPTH_2, D_MODEL, 2 * D_FF_2), D_MODEL),
        "w_down": w(ks[14], (DEPTH_2, D_FF_2, D_MODEL), D_FF_2),
        "g_post_ffn": gain(ks[15]),
    }

def second_block(x, mem, g_pre_mix, w_in, w_out, g_post_mix, g_pre_cross, g_mem, w_cq, w_ckv,
              w_co, g_post_cross, g_pre_ffn, w_gate_up, w_down, g_post_ffn):
    moba_inv = jnp.power(ROPE_THETA, -jnp.arange(ROPE_DIM // 2, dtype=jnp.float32) * 2.0 / ROPE_DIM)
    ret_inv = 1.0 / jnp.power(RET_THETA, jnp.linspace(0.0, 1.0, RET_QK_DIM // 2, dtype=jnp.float32))
    for l in range(DEPTH_2):
        h = rms_norm(x, g_pre_mix[l])
        proj = h @ w_in[l]
        mq, mk, mv, rq, rk, rv, rg = jnp.split(proj, SPLIT_POINTS, axis=-1)
        mq = rotary(split_heads(mq, MOBA_HEADS), moba_inv, ROPE_DIM)
        mk = rotary(split_heads(mk, MOBA_HEADS), moba_inv, ROPE_DIM)
        mo = merge_heads(moba_attention(mq, mk, split_heads(mv, MOBA_HEADS)))
        rq = rotary(split_heads(rq, RET_HEADS), ret_inv, RET_QK_DIM)
        rk = rotary(split_heads(rk, RET_HEADS), ret_inv, RET_QK_DIM) * (RET_QK_DIM ** -0.5)
        ro = retention(rq, rk, split_heads(rv, RET_HEADS))
        ro = ro * lax.rsqrt(jnp.mean(ro * ro, axis=-1, keepdims=True) + NORM_EPS)
        ro = jax.nn.silu(rg) * merge_heads(ro).astype(x.dtype)
        mix = jnp.concatenate([mo, ro], axis=-1) @ w_out[l]
        x = x + rms_norm(mix, g_post_mix[l])
        h = rms_norm(x, g_pre_cross[l])
        mem_n = rms_norm(mem, g_mem[l])
        c = cross_attention(h, mem_n, w_cq[l], w_ckv[l], w_co[l])
        x = x + rms_norm(c, g_post_cross[l])
        h = rms_norm(x, g_pre_ffn[l])
        gu = h @ w_gate_up[l]
        f = (jax.nn.silu(gu[..., :D_FF_2]) * gu[..., D_FF_2:]) @ w_down[l]
        x = x + rms_norm(f, g_post_ffn[l])
    return x


def setup_inputs(seed=0):
    out = dict(first_inputs(seed))
    for name, value in second_inputs(seed + 1).items():
        if name != "x":
            out[name + "_2"] = value
    return out


def reference(
    x, mem, norm_g, ffn_w_up, ffn_w_down, mem_norm_g, mem_w_kv, pool_w_in, pool_w_group,
    pool_scale, pool_w_out, diff_w_in, diff_lambda, diff_norm_g, diff_w_out, mlstm_w_in,
    mlstm_conv_w, mlstm_gate_b, mlstm_norm_g, mlstm_w_out, gla_w_in, gla_gate_w2, gla_gate_b,
    gla_norm_g, gla_w_out, final_norm_g, mem_2, g_pre_mix_2, w_in_2, w_out_2, g_post_mix_2,
    g_pre_cross_2, g_mem_2, w_cq_2, w_ckv_2, w_co_2, g_post_cross_2, g_pre_ffn_2, w_gate_up_2,
    w_down_2, g_post_ffn_2,
):
    x = first_block(
        x, mem, norm_g, ffn_w_up, ffn_w_down, mem_norm_g, mem_w_kv, pool_w_in, pool_w_group,
        pool_scale, pool_w_out, diff_w_in, diff_lambda, diff_norm_g, diff_w_out, mlstm_w_in,
        mlstm_conv_w, mlstm_gate_b, mlstm_norm_g, mlstm_w_out, gla_w_in, gla_gate_w2,
        gla_gate_b, gla_norm_g, gla_w_out, final_norm_g,
    )
    return second_block(
        x, mem_2, g_pre_mix_2, w_in_2, w_out_2, g_post_mix_2, g_pre_cross_2, g_mem_2, w_cq_2,
        w_ckv_2, w_co_2, g_post_cross_2, g_pre_ffn_2, w_gate_up_2, w_down_2, g_post_ffn_2,
    )


_drawn_inputs = setup_inputs


def setup_inputs(seed=0):
    import zlib

    import numpy as np

    out = dict(_drawn_inputs(seed))
    spreads = {}
    factors = {'mem_norm_g': 5.274, 'diff_norm_g': 3.784}
    for name, (base, spread) in spreads.items():
        noise = np.random.default_rng([zlib.crc32(name.encode()), seed]).standard_normal(out[name].shape)
        drawn = base * np.exp(spread * noise) if base else spread * noise
        out[name] = __import__('jax').numpy.asarray(drawn.astype(out[name].dtype))
    for name, factor in factors.items():
        out[name] = (out[name] * factor).astype(out[name].dtype)
    return out
```

```python
import math
from contextlib import ExitStack

import numpy as np

import concourse.bass as bass
from concourse import mybir

F32 = mybir.dt.float32
F32R = mybir.dt.float32r
ALU = mybir.AluOpType
ACT = mybir.ActivationFunctionType
AX = mybir.AxisListType

P = 128
D = 1024
S = 256
KT = D // P
D_FF = 2816
MID_TILES = D_FF // P
CHUNK = 2048
RAW = 3
RING = 3
COLS = CHUNK // KT
DFF_STEPS = MID_TILES // 2
LAM_INIT = 0.8 - 0.6 * math.exp(-0.3 * 1)
HEADS = 8
CAUSAL = ((0, 128), (128, 256))
FULL = ((0, 256), (256, 256))

GAINS = ["norm_g00", "norm_g01", "norm_g02", "norm_g10", "norm_g11", "norm_g12", "mem_norm_g",
         "pool_scale", "final_norm_g", "g_pre_mix", "g_post_mix", "g_pre_cross", "g_mem",
         "g_post_cross", "g_pre_ffn", "g_post_ffn"]
GAIN = {name: KT * n for n, name in enumerate(GAINS)}
DIFF_G = KT * len(GAINS)
N_VECS = DIFF_G + 1
TABLES = {}
_at = 0
for _name, _width in (("ident", P), ("ones", P), ("perm_moba", P), ("perm_ret", P), ("alibi", 384),
                      ("mask", 384), ("cos_moba", S), ("sin_moba", S), ("cos_ret", S),
                      ("sin_ret", S), ("inv_count", 4 * 16), ("decay", 4 * S), ("eps", 2)):
    TABLES[_name] = (_at, _width)
    _at += _width
N_TABLES = _at


def tables():
    t = np.zeros((P, N_TABLES), np.float32)

    def put(name, a):
        at, width = TABLES[name]
        t[:, at:at + width] = a

    p = np.arange(P)
    put("ident", np.eye(P))
    put("ones", 1.0)
    k = np.arange(S)[None, :] - (P + p)[:, None]
    alibi = np.where(k <= 0, k, -1e30)
    mask = np.where(k <= 0, 0.0, -1e30)
    put("alibi", np.concatenate([alibi[:, P:], alibi], 1))
    put("mask", np.concatenate([mask[:, P:], mask], 1))
    pos = np.arange(S, dtype=np.float64)[None, :]
    for name, rot, inv in (
            ("moba", 16, 500000.0 ** (-np.arange(8) * 2.0 / 16)),
            ("ret", 64, 1.0 / 10000.0 ** np.linspace(0.0, 1.0, 32))):
        half = rot // 2
        perm = np.zeros((P, P))
        cos, sin = np.ones((P, S)), np.zeros((P, S))
        for base in (0, 64):
            for i in range(half):
                a, b = base + i, base + half + i
                perm[b, a] = -1.0
                perm[a, b] = 1.0
                for r in (a, b):
                    cos[r] = np.cos(pos * inv[i])
                    sin[r] = np.sin(pos * inv[i])
        put("perm_" + name, perm)
        put("cos_" + name, cos)
        put("sin_" + name, sin)
    inv_count = [1.0 / np.minimum(np.arange(1, 17), w) for w in (2, 4, 8, 16)]
    put("inv_count", np.concatenate(inv_count)[None, :])
    decay = []
    for h in range(4):
        lg = np.log(1.0 - 2.0 ** (-5.0 - h))
        d = np.arange(S)[None, :] - p[:, None]
        decay.append(np.where(d >= 0, np.exp(lg * np.maximum(d, 0)), 0.0) * 64 ** -0.5)
    put("decay", np.concatenate(decay, 1))
    put("eps", np.array([1e-6, 1e-5])[None, :])
    return t


class Plan:

    def __init__(self):
        self.items = []
        self.chunks = []
        self.c = self.e = self.m = self.y = self.j = self.u = self.aux = 0
        self.acts = 0
        self.x_new = 0
        self.mixed = 0
        self.tile_at = {}
        self.stat = 0
        self.rope_n = 0
        self.y_chunk = 0
        self.acc_taken = None
        self.y_copied = 0
        self.acts_users = 0
        self.hn = 0
        self.rg = 0

    def add(self, kind, **k):
        k["kind"] = kind
        self.items.append(k)
        return k

    def chunk(self, kind, source, **k):
        self.chunks.append(source)
        item = self.add(kind, c=self.c, **k)
        self.c += 1
        if kind in ("cols", "rows_out"):
            self.acts_users = self.c
            item["e"] = self.e
            self.e += 1
        return item

    def statistic(self, src, eps, width, **k):
        self.add("stat", n=self.stat, src=src, eps=eps, width=width, aux=self.aux, **k)
        self.stat += 1
        self.aux += 1

    def prep(self, src, gain, resid=None, after_chunk=True):
        first = self.acts
        self.add("prep", src=src, gain=gain, resid=resid, first=first, acts_free=self.acts_users,
                 x_new=self.x_new, y=self.y, y_chunk=self.y_chunk)
        if resid is not None:
            self.x_new += 4
            self.acc_taken = ("x_new", self.x_new)
        self.acts += KT
        self.statistic(src, 0, D, after_chunk=after_chunk, x_new=self.x_new)

    def residual(self, scale):
        self.add("residual", scale=scale, y=self.y, y_chunk=self.y_chunk, x_new=self.x_new)
        self.x_new += 4
        self.acc_taken = ("x_new", self.x_new)

    def post_norm_sums(self):
        self.add("post_norm_sums", y=self.y, y_chunk=self.y_chunk)
        self.y_copied += 4
        self.acc_taken = ("y_copied", self.y_copied)

    def down(self, source_name, idx, pairs):
        for n, pair in enumerate(pairs):
            self.chunk("down", (source_name, idx, "rows", pair), pair=pair, first=(n == 0),
                       last=(n == len(pairs) - 1), mixed=max(self.tile_at[2 * pair], self.tile_at[2 * pair + 1]),
                       j=self.j, u=self.u, acc_taken=self.acc_taken)
        self.y += 3
        self.y_chunk = self.c

    def ffn(self, up, down, idx):
        item = self.add("ffn", c=self.c, e=self.e, m=self.m, y=self.y, acts=self.acts, acc_taken=self.acc_taken, j=self.j, u=self.u)
        for p in range(3 * DFF_STEPS):
            kind, i = ffn_step(p)
            self.chunks.append((up, idx, "gate_up", i) if kind == "up" else (down, idx, "rows", i))
        self.c += 3 * DFF_STEPS
        self.e += MID_TILES
        self.m += MID_TILES
        self.acts_users = self.c - 2
        self.y += 3
        self.y_chunk = self.c
        return item

    def project(self, source, col, dest, at, tokens_out=False, **k):
        return self.chunk("rows_out" if tokens_out else "cols", (*source, "cols", col), dest=dest,
                          at=at, acts=self.acts, **k)

    def ticks(self, units):
        subs = []
        for unit in units:
            for comp in range(unit["comps"]):
                subs.append((unit, comp))
        made, transposed = [], None
        for k in range(len(subs) + 2):
            tick = {"S": None, "F": None, "T": None, "V": transposed}
            if k < len(subs):
                unit, comp = subs[k]
                while unit["need"] is None:
                    yield "blocked"
                if comp == 0:
                    unit["u"] = self.u
                    self.u += 1
                tick["S"] = (unit, comp, self.j)
                tick["acc_taken"] = self.acc_taken
                made.append((unit, comp, self.j))
                self.j += 1
            if 1 <= k <= len(subs):
                tick["F"] = made[k - 1]
                unit, comp, j = made[k - 1]
                if comp == unit["comps"] - 1:
                    tick["T"] = (unit, j)
            if transposed is not None:
                unit = transposed[0]
                if unit["out"] == "mix":
                    for n in range(unit["out_tiles"]):
                        self.mixed += 1
                        self.tile_at[unit["tile"] + n] = self.mixed
                    unit["mixed_at"] = self.mixed
            transposed = tick["T"]
            self.add("tick", **tick)
            yield

    def head_norm(self, pair, which):
        self.add("head_norm", pair=pair, which=which, n=self.hn, aux=self.aux, units=self.u)
        self.hn += 1
        self.aux += 1
        for n in range(2):
            self.mixed += 1
            self.tile_at[HN_TILE[which] + 2 * pair + n] = self.mixed

    def rope(self, dest, at, which, e):
        self.add("rope", dest=dest, at=at, which=which, e=e, aux=self.aux)
        self.aux += 1
        self.rope_n += 1


HN_TILE = {"diff": 0, "ret": 4}


def ffn_step(p):
    if p < 2:
        return "up", p
    i, r = 1 + (p - 2) // 3, (p - 2) % 3
    if i == DFF_STEPS:
        return "down", DFF_STEPS - 1
    return ("up", 2 * i + r) if r < 2 else ("down", i - 1)


def interleave(ticks, n):
    for _ in range(n):
        if next(ticks, "end") is not None:
            return


def mem_units(heads, dims, q, need, scale):
    tiles = dims // P
    return [dict(comps=1, shape=FULL, table=None, scale=scale, q=(q, h * tiles), k=("mem_k", h * tiles),
                 rows=(0, P), tiles=tiles, v=("mem_v", h * dims), v_width=P, out="mix", out_tiles=tiles,
                 tile=(8 if tiles == 1 else 0) + h * tiles, out_row=0, need=need, rope=0, head=h)
            for h in range(heads)]


def make_plan():
    pl = Plan()
    pl.add("lambda")

    def kv(layer):
        for n in range(2):
            pl.project(("mem_w_kv", layer), n * COLS, "mem_k", 2 * n)
        for n in range(2):
            pl.project(("mem_w_kv", layer), 512 + n * COLS, "mem_v", n * COLS, tokens_out=True)

    pl.prep("x", "norm_g00")
    pl.ffn("ffn_w_up", "ffn_w_down", (0, 0))
    pl.prep("mem", "mem_norm_g")
    pl.residual(0.5)
    kv(0)
    pl.prep("x", "norm_g01")
    for n in range(2):
        pl.project(("pool_w_in", 0), D + n * COLS, "xq", 2 * n)
    ticks = pl.ticks(mem_units(4, P, "xq", pl.e, P ** -0.5))
    for n in range(4):
        pl.project(("pool_w_in", 0), n * COLS, "u", 2 * n)
        interleave(ticks, 2)
    interleave(ticks, 99)
    pl.add("pool", e=pl.e, first=pl.acts, acts_free=pl.acts_users)
    pl.acts += KT
    n_down = [4, 5, 0, 1, 2, 3]
    pl.chunk("down", ("pool_w_out", 0, "rows", 4), pair=4, first=True, last=False,
             mixed=max(pl.tile_at[8], pl.tile_at[9]), j=pl.j, u=pl.u, acc_taken=pl.acc_taken)
    pl.chunk("down", ("pool_w_out", 0, "rows", 5), pair=5, first=False, last=False,
             mixed=max(pl.tile_at[10], pl.tile_at[11]), j=pl.j, u=pl.u, acc_taken=pl.acc_taken)
    g = pl.chunk("group", ("pool_w_group", 0, "group", 0), e=pl.e, acts=pl.acts)
    for t in range(8):
        pl.mixed += 1
        pl.tile_at[t] = pl.mixed
    for n, pair in enumerate(n_down[2:]):
        pl.chunk("down", ("pool_w_out", 0, "rows", pair), pair=pair, first=False, last=(n == 3),
                 mixed=pl.tile_at[2 * pair + 1], j=pl.j, u=pl.u, acc_taken=pl.acc_taken)
    pl.y += 3
    pl.y_chunk = pl.c
    pl.prep("x", "norm_g02", resid=1.0)
    pl.ffn("ffn_w_up", "ffn_w_down", (0, 1))
    pl.prep("x", "norm_g10", resid=0.5)
    pl.ffn("ffn_w_up", "ffn_w_down", (1, 0))
    pl.prep("mem", "mem_norm_g")
    pl.residual(0.5)
    kv(1)
    pl.prep("x", "norm_g11")
    for n in range(2):
        pl.project(("diff_w_in", 0), 3 * D + n * COLS, "xq", 2 * n)
    mem_ticks = pl.ticks(mem_units(4, P, "xq", pl.e, P ** -0.5))
    slopes = [2.0 ** (-8.0 * (h + 1) / HEADS) for h in range(HEADS)]
    diff_units = [dict(comps=2, shape=CAUSAL, table="alibi", slope=slopes[h], scale=64 ** -0.5, q=("q", h),
                       k=("k", h), rows=None, tiles=1, v=("v", h * P), v_width=P, out="obuf", out_tiles=1,
                       tile=h, out_row=0, need=None, rope=0, head=h) for h in range(HEADS)]

    def chain(*gens):
        for one in gens:
            yield from one

    all_ticks = chain(mem_ticks, pl.ticks(diff_units))
    normed = 0

    def norms(n):
        out = [i["V"][0]["tile"] for i in pl.items
               if i["kind"] == "tick" and i["V"] and i["V"][0]["out"] == "obuf"]
        while n < 4 and 2 * n + 1 in out:
            pl.head_norm(n, "diff")
            n += 1
        return n

    for pair in range(4):
        pl.project(("diff_w_in", 0), pair * COLS, "q", 2 * pair)
        interleave(all_ticks, 2)
        pl.project(("diff_w_in", 0), D + pair * COLS, "k", 2 * pair)
        interleave(all_ticks, 2)
        pl.project(("diff_w_in", 0), 2 * D + pair * COLS, "v", pair * COLS, tokens_out=True)
        for h in (2 * pair, 2 * pair + 1):
            diff_units[h]["need"] = pl.e
        interleave(all_ticks, 1 if pair == 0 else 2)
        normed = norms(normed)
    while next(all_ticks, "end") != "end":
        normed = norms(normed)
    pl.down("diff_w_out", 0, [4, 5, 0, 1, 2, 3])
    pl.prep("x", "norm_g12", resid=1.0)
    pl.ffn("ffn_w_up", "ffn_w_down", (1, 1))
    pl.residual(0.5)
    pl.statistic("x", 0, D, after_chunk=False, x_new=pl.x_new)
    pl.add("final_norm", gain="final_norm_g", x_new=pl.x_new)
    pl.x_new += 4
    pl.prep("x", "g_pre_mix")
    w = ("w_in_2", 0)
    pl.project(w, 1536, "k", 4)
    pl.rope("k", 4, "ret", pl.e)
    pl.project(w, 1792, "k", 6)
    pl.rope("k", 6, "ret", pl.e)
    need_rope = pl.rope_n
    for n in range(2):
        pl.project(w, 2048 + n * COLS, "v", 512 + n * COLS, tokens_out=True)
    ret_units = [dict(comps=1, shape=CAUSAL, table="decay", scale=1.0, q=("k", 4 + h // 2), k=("k", 6 + h // 2),
                      rows=(64 * (h % 2), 64 * (h % 2) + 64), tiles=1, v=("v", 512 + h * P), v_width=P, out="obuf",
                      out_tiles=1, tile=h, out_row=0, need=pl.e, rope=need_rope, head=h) for h in range(4)]
    ticks = pl.ticks(ret_units)
    for n in range(2):
        pl.project(w, 2560 + n * COLS, "rg", 2 * n)
        pl.add("gate_silu", e=pl.e, at=2 * n, n=n)
        interleave(ticks, 2)
    first = True
    for half in range(2):
        pl.project(w, half * COLS, "q", 2 * half)
        pl.rope("q", 2 * half, "moba", pl.e)
        interleave(ticks, 2)
        if half == 0:
            pl.head_norm(0, "ret")
            pl.head_norm(1, "ret")
            pl.add("load_mem2", hn=pl.hn)
        pl.project(w, 512 + half * COLS, "k", 2 * half)
        pl.rope("k", 2 * half, "moba", pl.e)
        interleave(ticks, 2)
        pl.project(w, 1024 + half * COLS, "v", half * COLS, tokens_out=True)
        units = [dict(comps=1, shape=CAUSAL, table="mask", slope=None, scale=64 ** -0.5, q=("q", h // 2),
                      k=("k", h // 2), rows=(64 * (h % 2), 64 * (h % 2) + 64), tiles=1, v=("v", 64 * h),
                      v_width=64, out="mix", out_tiles=1, tile=h // 2, out_row=64 * (h % 2), need=pl.e,
                      rope=pl.rope_n, head=h) for h in range(4 * half, 4 * half + 4)]
        interleave(ticks, 99)
        ticks = pl.ticks(units)
        interleave(ticks, 2)
    interleave(ticks, 99)
    pl.prep("mem", "g_mem")
    pl.down("w_out_2", 0, [2, 3, 0, 1])
    pl.post_norm_sums()
    pl.statistic("y", 0, D, after_chunk=True, x_new=0)
    for n in range(4):
        pl.project(("w_ckv_2", 0), n * COLS, "mem_k", 2 * n)
        if n == 1:
            pl.add("post_norm", gain="g_post_mix", x_new=pl.x_new)
            pl.x_new += 4
    for n in range(4):
        pl.project(("w_ckv_2", 0), D + n * COLS, "mem_v", n * COLS, tokens_out=True)
    pl.prep("x", "g_pre_cross")
    ticks = None
    for n in range(4):
        pl.project(("w_cq_2", 0), n * COLS, "q", 2 * n)
        if n == 0:
            units = mem_units(4, 2 * P, "q", None, (2 * P) ** -0.5)
            ticks = pl.ticks(units)
        units[n]["need"] = pl.e
        interleave(ticks, 1)
    interleave(ticks, 99)
    pl.down("w_co_2", 0, [0, 1, 2, 3])
    pl.post_norm_sums()
    pl.statistic("y", 0, D, after_chunk=False, x_new=0)
    pl.add("post_norm", gain="g_post_cross", x_new=pl.x_new)
    pl.x_new += 4
    pl.prep("x", "g_pre_ffn")
    pl.ffn("w_gate_up_2", "w_down_2", 0)
    pl.post_norm_sums()
    pl.statistic("y", 0, D, after_chunk=False, x_new=0)
    pl.add("post_norm", gain="g_post_ffn", x_new=pl.x_new)
    pl.x_new += 4
    pl.add("store", x_new=pl.x_new)
    return pl


def columns(a):
    return np.asarray(a).reshape(-1, P).T


def features_first(a):
    return np.ascontiguousarray(np.asarray(a)[0].T.reshape(KT, P, S).transpose(1, 0, 2))


def lay_out_chunk(inputs, source, out):
    name, idx, how, at = source
    w = inputs[name][idx]
    if how == "gate_up":
        v = w.reshape(KT, P, 2, D_FF)[:, :, :, at * P:(at + 1) * P].transpose(1, 0, 2, 3)
        out.reshape(P, KT, 2, P)[...] = v
    elif how == "cols":
        v = w.reshape(KT, P, -1)[:, :, at:at + COLS].transpose(1, 0, 2)
        out.reshape(P, KT, COLS)[...] = v
    elif how == "rows":
        v = w[2 * P * at:2 * P * (at + 1)].reshape(2, P, D).transpose(1, 0, 2)
        out.reshape(P, 2, D)[...] = v
    else:
        out.reshape(P, 8, COLS)[...] = w.reshape(8, P, COLS).transpose(1, 0, 2)


def build(nc, A, plan):
    items = plan.items
    N = plan.c
    assert len(plan.chunks) == N

    with ExitStack() as ctx:
        def sb(name, shape, dt=F32):
            return ctx.enter_context(nc.sbuf_tensor(name, shape, dt))

        def sem(name):
            return ctx.enter_context(nc.semaphore(name))

        raw = sb("raw", [P, RAW, CHUNK])
        w_hi = sb("w_hi", [P, RING, CHUNK], F32R)
        w_lo = sb("w_lo", [P, RING, CHUNK], F32R)
        x = sb("x_res", [P, KT, S])
        acts_h = sb("acts_h", [P, KT, S], F32R)
        acts_l = sb("acts_l", [P, KT, S], F32R)
        mix_h = sb("mix_h", [P, 12, S], F32R)
        mix_l = sb("mix_l", [P, 12, S], F32R)
        mem_k = sb("mem_k", [P, KT, S])
        mem_v = sb("mem_v", [P, 2, D])
        work = sb("work", [P, 3 * KT * S])
        xq = sb("xq", [P, 4, S])
        mem_x = sb("mem_x", [P, KT, S])
        sq = sb("sq", [P, KT, S])
        four = sb("four", [P, 4, 512])
        masked = sb("masked", [P, 2, 384])
        rstd = sb("rstd", [P, 2, S + 2])
        small = sb("small", [P, 2, 8])
        lam = sb("lam", [P, 12])
        vecs = sb("vecs", [P, N_VECS])
        tabs = sb("tabs", [P, N_TABLES])

        q_t = work[:, 0:KT * S].rearrange("p (k t) -> p k t", t=S)
        k_t = work[:, KT * S:2 * KT * S].rearrange("p (k t) -> p k t", t=S)
        v_flat = work[:, 2 * KT * S:3 * KT * S]
        v_t = v_flat.rearrange("p (t n) -> p t n", t=2)
        ybuf = v_flat.rearrange("p (k t) -> p k t", t=S)
        PAD = 16
        padded = work[:, 0:KT * (S + PAD)].rearrange("p (k t) -> p k t", t=S + PAD)
        shifted = [work[:, 2176 + 544 * n:2176 + 544 * (n + 1)].rearrange("p (k t) -> p k t", t=S + PAD)
                   for n in range(2)]
        obuf = mem_x
        dests = {"q": q_t, "k": k_t, "xq": xq[:], "rg": xq[:], "mem_k": mem_k[:]}
        tok_dests = {"v": v_t, "mem_v": mem_v[:]}
        sources = {"x": x[:], "mem": mem_x[:], "y": ybuf}
        hn_sq = sq[:, 0:2, :]
        hn_root = sq[:, 2:4, :]
        hn_on = sq[:, 4:6, :]
        sums = four[:, 0, 0:S]
        lamb = sq[:, 4, :].rearrange("p (a b c) -> p a b c", a=2, b=2)

        def table(name):
            at, width = TABLES[name]
            return tabs[:, at:at + width]

        def gain_col(name, kt):
            at = GAIN[name] + kt
            return vecs[:, at:at + 1]

        eps_col = {0: table("eps")[:, 0:1], 1: table("eps")[:, 1:2]}
        ident, ones = table("ident"), table("ones")

        acc = [ctx.enter_context(nc.psum_tensor(f"acc{b}", [P, 2, S], F32)) for b in range(4)]
        prod = [ctx.enter_context(nc.psum_tensor(f"prod{b}", [P, 2, S], F32)) for b in range(2)]
        aux = ctx.enter_context(nc.psum_tensor("aux", [P, 512], F32))
        o_bank = ctx.enter_context(nc.psum_tensor("o_bank", [P, 2, S], F32))
        score = [acc[b][:].rearrange("p a b -> p (a b)") for b in (0, 1)]
        p_turned = [acc[b][:].rearrange("p a b -> p (a b)") for b in (2, 3)]

        raw_loaded = [sem(f"raw_loaded{n}") for n in range(RAW)]
        small_loaded = sem("small_loaded")
        mem_loaded = sem("mem_loaded")
        hi_done = sem("hi_done")
        lo_done = sem("lo_done")
        chunk_used = sem("chunk_used")
        group_done = sem("group_done")
        prod_read = sem("prod_read")
        silu_done = sem("silu_done")
        mid_done = sem("mid_done")
        mid_hi = sem("mid_hi")
        mid_lo = sem("mid_lo")
        acc_done = sem("acc_done")
        x_new = sem("x_new")
        acts_hi = sem("acts_hi")
        acts_lo = sem("acts_lo")
        y_copied = sem("y_copied")
        squared = sem("squared")
        summed = sem("summed")
        aux_done = sem("aux_done")
        rooted = sem("rooted")
        score_done = sem("score_done")
        decayed = sem("decayed")
        max_done = sem("max_done")
        exp_done = sem("exp_done")
        weights_done = sem("weights_done")
        turned = sem("turned")
        turned_read = sem("turned_read")
        o_done = sem("o_done")
        o_hi = sem("o_hi")
        o_copied = sem("o_copied")
        mix_hi = sem("mix_hi")
        mixed = sem("mixed")
        hn_squared = sem("hn_squared")
        hn_rooted = sem("hn_rooted")
        hn_scaled = sem("hn_scaled")
        roped = sem("roped")
        pooled = sem("pooled")
        gated = sem("gated")
        lam_part = sem("lam_part")
        act_step = sem("act_step")
        dve_step = sem("dve_step")
        stored = sem("stored")

        by_name = {"x_new": x_new, "y_copied": y_copied, "exp_done": exp_done, "decayed": decayed,
                   "rooted": rooted, "hn_rooted": hn_rooted, "roped": roped, "mixed": mixed,
                   "o_copied": o_copied}

        def reader(engine, told):
            if told:
                engine.wait_ge(by_name[told[0]], told[1])

        block = ctx.enter_context(nc.Block())

        def bcast(ap, n):
            return ap.unsqueeze(1).broadcast_to([P, n, S])

        @block.sync
        def _(sp):
            weights = A["weights"]
            for n in range(RAW):
                sp.dma_start(raw[:, n], weights[n]).then_inc(raw_loaded[n], 16)
            turns = (N - RAW) // RAW
            with sp.Fori(0, turns, 1) as i:
                for n in range(RAW):
                    sp.wait_ge(lo_done, i * RAW + n + 1)
                    sp.dma_start(raw[:, n], weights[bass.ds(i * RAW + n + RAW, 1)].rearrange("o p f -> (o p) f")
                                 ).then_inc(raw_loaded[n], 16)
            for c in range(RAW * (turns + 1), N):
                sp.wait_ge(lo_done, c - RAW + 1)
                sp.dma_start(raw[:, c % RAW], weights[c]).then_inc(raw_loaded[c % RAW], 16)

        @block.gpsimd
        def _(pool):
            pool.dma_start(x[:], A["x"]).then_inc(small_loaded, 16)
            pool.dma_start(vecs[:], A["vecs"]).then_inc(small_loaded, 16)
            pool.dma_start(tabs[:], A["tabs"]).then_inc(small_loaded, 16)
            pool.dma_start(lamb, A["lambda"]).then_inc(small_loaded, 16)
            pool.dma_start(mem_x[:], A["mem"]).then_inc(mem_loaded, 16)
            for it in items:
                if it["kind"] == "load_mem2":
                    pool.wait_ge(mixed, it["mixed"])
                    pool.dma_start(mem_x[:], A["mem2"]).then_inc(mem_loaded, 16)
                elif it["kind"] == "store":
                    pool.wait_ge(x_new, it["x_new"])
                    pool.dma_start(A["out"], x[:]).then_inc(stored, 16)
                    pool.wait_ge(stored, 16)

        @block.tensor
        def _(pe):
            seen = {"acts": 0}

            def passes(out, w, moving_hi, moving_lo, slot, first, last):
                pe.matmul(out, w(w_hi, slot), moving_hi, start=first, stop=False, skip_group_check=True)
                pe.matmul(out, w(w_hi, slot), moving_lo, start=False, stop=False, skip_group_check=True)
                return pe.matmul(out, w(w_lo, slot), moving_hi, start=False, stop=last, skip_group_check=True)

            def columns_chunk(slot, bank, acts):
                for kt in range(KT):
                    if acts is not None and seen["acts"] < acts:
                        pe.wait_ge(acts_lo, acts - KT + kt + 1)
                    for half in range(2):
                        mm = passes(prod[bank][:, half],
                                    lambda w, s, a=kt * COLS + half * P: w[:, s, a:a + P],
                                    acts_h[:, kt], acts_l[:, kt], slot, kt == 0 and half == 0, kt == KT - 1)
                if acts is not None:
                    seen["acts"] = max(seen["acts"], acts)
                return mm

            def tokens_chunk(slot, bank, acts):
                if seen["acts"] < acts:
                    pe.wait_ge(acts_lo, acts)
                    seen["acts"] = acts
                for t in range(2):
                    for kt in range(KT):
                        a_h = acts_h[:, kt, t * P:(t + 1) * P]
                        a_l = acts_l[:, kt, t * P:(t + 1) * P]
                        wh = w_hi[:, slot, kt * COLS:(kt + 1) * COLS]
                        wl = w_lo[:, slot, kt * COLS:(kt + 1) * COLS]
                        out = prod[bank][:, t]
                        pe.matmul(out, a_h, wh, start=(kt == 0), stop=False, skip_group_check=True)
                        pe.matmul(out, a_h, wl, start=False, stop=False, skip_group_check=True)
                        mm = pe.matmul(out, a_l, wh, start=False, stop=(kt == KT - 1), skip_group_check=True)
                return mm

            def down_chunk(slot, tiles, first, last):
                for b in range(4):
                    for n, tile in enumerate(tiles):
                        for half in range(2):
                            a = n * D + (2 * b + half) * P
                            mm = passes(acc[b][:, half], lambda w, s, a=a: w[:, s, a:a + P], mix_h[:, tile],
                                        mix_l[:, tile], slot, first and n == 0 and half == 0, last and n == 1)
                    if last and b < 3:
                        mm.then_inc(acc_done, 1)
                mm.then_inc(chunk_used, 1)

            def statistic(it):
                pe.wait_ge(summed, it["n"] + 1)
                reader(pe, it["aux_reader"])
                pe.matmul(aux[:, 0:S], ones, sums, start=True, stop=True)
                pe.matmul(aux[:, S:S + 1], sums[:, 0:P], ones[:, 0:1], start=True, stop=True)
                pe.matmul(aux[:, S + 1:S + 2], sums[:, P:2 * P], ones[:, 0:1], start=True,
                          stop=True).then_inc(aux_done, 1)

            def ffn_part(it, p, turn):
                kind, i = ffn_step(p)
                c = it["c"] + p
                pe.wait_ge(lo_done, turn * 6 + c + 1)
                if kind == "up":
                    e = it["e"] + i
                    if e >= 2:
                        pe.wait_ge(prod_read, turn * 4 + e - 1)
                    columns_chunk(c % RING, e % 2, it["acts"]).then_inc(chunk_used, 1)
                else:
                    pe.wait_ge(mid_lo, turn * 4 + it["m"] + 2 * i + 2)
                    if i == 0:
                        free_accumulators(it)
                    down_chunk(c % RING, [(2 * i) % 4, (2 * i + 1) % 4], i == 0, i == DFF_STEPS - 1)

            def free_accumulators(it):
                reader(pe, it["acc_taken"])
                for j in (it["j"] - 2, it["j"] - 1):
                    reader(pe, plan.score_reader.get(j))
                if it["t"]:
                    pe.wait_ge(turned_read, it["t"])

            def tick(it):
                if it["S"]:
                    unit, comp, j = it["S"]
                    pe.wait_ge(prod_read, unit["need"])
                    if unit["rope"]:
                        pe.wait_ge(roped, unit["rope"])
                    reader(pe, it["acc_taken"])
                    reader(pe, plan.score_reader.get(j - 2))
                    r0, r1 = unit["rows"] or (64 * comp, 64 * comp + 64)
                    q, qt = unit["q"]
                    k, kt = unit["k"]
                    bank = score[j % 2]
                    if unit["table"] == "decay":
                        for t, (at, width) in enumerate(((0, 256), (256, 128))):
                            mm = pe.matmul(bank[:, at:at + width], dests[k][r0:r1, kt, t * P:(t + 1) * P],
                                           dests[q][r0:r1, qt, S - width:S], start=True, stop=True)
                    else:
                        for t, (at, width) in enumerate(unit["shape"]):
                            for n in range(unit["tiles"]):
                                mm = pe.matmul(bank[:, at:at + width],
                                               dests[q][r0:r1, qt + n, t * P:(t + 1) * P],
                                               dests[k][r0:r1, kt + n, 0:width], start=(n == 0),
                                               stop=(n == unit["tiles"] - 1))
                    mm.then_inc(score_done, 1)
                if it["T"] and it["T"][0]["table"] != "decay":
                    unit, j = it["T"]
                    pe.wait_ge(weights_done, unit["t"])
                    bank = p_turned[unit["u"] % 2]
                    for t, (at, width) in enumerate(unit["shape"]):
                        for m in range(width // P):
                            mm = pe.transpose(bank[:, m * S + t * P:m * S + (t + 1) * P],
                                              four[:, j % 2, at + m * P:at + (m + 1) * P], ident)
                    mm.then_inc(turned, 1)
                if it["V"]:
                    unit, j = it["V"]
                    v, col = unit["v"]
                    vt = tok_dests[v]
                    w = unit["v_width"]
                    decay = unit["table"] == "decay"
                    if decay:
                        pe.wait_ge(decayed, unit["d"])
                    else:
                        pe.wait_ge(turned_read, unit["t"])
                    reader(pe, plan.o_reader.get(unit["u"] - 1))
                    for n in range(unit["out_tiles"]):
                        c = col + n * P
                        out = o_bank[unit["out_row"]:unit["out_row"] + w, n]
                        if unit["shape"] is FULL:
                            pe.matmul(out, vt[:, 0, c:c + w], four[:, 2 + unit["u"] % 2, 0:S], start=True, stop=False)
                            mm = pe.matmul(out, vt[:, 1, c:c + w], four[:, 2 + unit["u"] % 2, S:2 * S], start=False,
                                           stop=True)
                        else:
                            src = four[:, j % 2, :] if decay else four[:, 2 + unit["u"] % 2, :]
                            late = src[:, S:S + P] if decay else src[:, S + P:2 * S]
                            pe.matmul(out, vt[:, 0, c:c + w], src[:, 0:S], start=True, stop=False,
                                      skip_group_check=True)
                            mm = pe.matmul(out[:, P:S], vt[:, 1, c:c + w], late, start=False, stop=True,
                                           skip_group_check=True)
                    mm.then_inc(o_done, 1)

            pe.wait_ge(small_loaded, 64)
            late_statistic = None
            for it in items:
                kind = it["kind"]
                if kind == "ffn":
                    for p in range(5):
                        ffn_part(it, p, 0)
                        if p == 0 and late_statistic:
                            statistic(late_statistic)
                            late_statistic = None
                    with pe.Fori(0, 4, 1) as turn:
                        for p in range(5, 11):
                            ffn_part(it, p, turn)
                    for p in range(29, 33):
                        ffn_part(it, p, 0)
                elif kind in ("cols", "rows_out", "down", "group"):
                    c = it["c"]
                    pe.wait_ge(lo_done, c + 1)
                    if kind in ("cols", "rows_out"):
                        if it["e"] >= 2:
                            pe.wait_ge(prod_read, it["e"] - 1)
                        part = columns_chunk if kind == "cols" else tokens_chunk
                        part(c % RING, it["e"] % 2, it["acts"]).then_inc(chunk_used, 1)
                    elif kind == "down":
                        pe.wait_ge(mixed, it["mixed"])
                        if it["first"]:
                            free_accumulators(it)
                        down_chunk(c % RING, [2 * it["pair"], 2 * it["pair"] + 1], it["first"], it["last"])
                    else:
                        pe.wait_ge(acts_lo, it["acts"])
                        for g in range(4):
                            e = it["e"] + g
                            if g < 2:
                                pe.wait_ge(prod_read, e - 1)
                            else:
                                pe.wait_ge(mixed, it["mixed"] + 2 * (g - 1))
                            for half in range(2):
                                for n in range(2):
                                    a = (2 * g + n) * COLS + half * P
                                    mm = passes(prod[e % 2][:, half], lambda w, s, a=a: w[:, s, a:a + P],
                                                acts_h[:, 2 * g + n], acts_l[:, 2 * g + n], c % RING,
                                                n == 0, n == 1)
                            mm.then_inc(group_done if g < 3 else chunk_used, 1)
                    if late_statistic:
                        statistic(late_statistic)
                        late_statistic = None
                elif kind == "stat":
                    if it["after_chunk"]:
                        late_statistic = it
                    else:
                        statistic(it)
                elif kind == "tick":
                    tick(it)
                elif kind == "rope":
                    pe.wait_ge(prod_read, it["e"])
                    reader(pe, it["aux_reader"])
                    pe.matmul(aux[:], table("perm_" + it["which"]),
                              dests[it["dest"]][:, it["at"]:it["at"] + 2, :].rearrange("p a b -> p (a b)"),
                              start=True, stop=True).then_inc(aux_done, 1)
                elif kind == "head_norm":
                    pe.wait_ge(hn_squared, it["n"] + 1)
                    reader(pe, it["aux_reader"])
                    pe.matmul(aux[:], ones, hn_sq.rearrange("p a b -> p (a b)"), start=True,
                              stop=True).then_inc(aux_done, 1)

        @block.scalar
        def _(act):
            state = {"split": 0, "target": RING, "own": 0}

            def split(c, turn=0):
                if c >= N:
                    return
                act.wait_ge(raw_loaded[c % RAW], turn * (16 * 6 // RAW) + 16 * (c // RAW + 1))
                if c >= RING:
                    act.wait_ge(chunk_used, turn * 6 + c - RING + 1)
                act.copy(w_hi[:, c % RING], raw[:, c % RAW]).then_inc(hi_done, 1)

            def flush(upto=None):
                upto = state["target"] if upto is None else upto
                while state["split"] < min(upto, N):
                    split(state["split"])
                    state["split"] += 1

            def own(ins):
                ins.then_inc(act_step, 1)
                state["own"] += 1
                act.wait_ge(act_step, state["own"])

            def ffn_part(it, p, turn, split_too=True):
                kind, i = ffn_step(p)
                c = it["c"] + p
                m = it["m"] + i
                if kind == "up":
                    act.wait_ge(prod_read, turn * 4 + it["e"] + i + 1)
                    act.activation(four[:, 2, (m % 2) * S:(m % 2 + 1) * S], four[:, m % 2, 0:S],
                                   ACT.Silu).then_inc(silu_done, 1)
                if split_too:
                    split(c + RING, turn)
                if kind == "up":
                    act.wait_ge(mid_done, turn * 4 + m + 1)
                    act.copy(mix_h[:, i % 4], four[:, 3, (m % 2) * S:(m % 2 + 1) * S]).then_inc(mid_hi, 1)

            act.wait_ge(small_loaded, 64)
            flush()
            for it in items:
                kind = it["kind"]
                if kind == "ffn":
                    flush()
                    assert state["split"] == it["c"] + RING
                    for p in range(5):
                        ffn_part(it, p, 0)
                    with act.Fori(0, 4, 1) as turn:
                        for p in range(5, 11):
                            ffn_part(it, p, turn)
                    for p in range(29, 33):
                        ffn_part(it, p, 0, split_too=(p < 31))
                    state["split"] = it["c"] + 31 + RING
                    state["target"] = it["c"] + 33 + RING
                elif kind in ("cols", "rows_out", "down", "group"):
                    flush()
                    if kind == "group":
                        for g in range(4):
                            if g < 3:
                                act.wait_ge(group_done, g + 1)
                            else:
                                act.wait_ge(chunk_used, it["c"] + 1)
                            for half in range(2):
                                act.activation(mix_h[:, 2 * g + half], prod[(it["e"] + g) % 2][:, half], ACT.Copy,
                                               scale=gain_col("pool_scale", 2 * g + half)).then_inc(mix_hi, 1)
                    state["target"] = it["c"] + 1 + RING
                elif kind == "prep":
                    if it["resid"] is not None:
                        flush(state["target"] - 1)
                    if it["src"] == "mem":
                        act.wait_ge(mem_loaded, it["mem_loaded"])
                    if it["acts_free"]:
                        act.wait_ge(chunk_used, it["acts_free"])
                    if it["first"]:
                        act.wait_ge(acts_lo, it["first"])
                    for kt in range(KT):
                        if it["src"] == "x":
                            if it["resid"] is not None:
                                act.wait_ge(x_new, it["x_new"] + kt // 2 + 1)
                            elif it["x_new"]:
                                act.wait_ge(x_new, it["x_new"])
                        act.activation(acts_h[:, kt], sources[it["src"]][:, kt], ACT.Copy,
                                       scale=gain_col(it["gain"], kt)).then_inc(acts_hi, 1)
                elif kind == "post_norm_sums":
                    pass
                elif kind == "stat":
                    if it["src"] == "y":
                        act.wait_ge(y_copied, it["y_copied"])
                    elif it["src"] == "x" and it["x_new"]:
                        act.wait_ge(x_new, it["x_new"])
                    if it["n"]:
                        act.wait_ge(summed, it["n"])
                    if it["hn"]:
                        act.wait_ge(hn_scaled, it["hn"])
                        act.wait_ge(mixed, it["mixed"])
                    act.activation(sq[:], sources[it["src"]], ACT.Square).then_inc(squared, 1)
                    flush()
                    act.wait_ge(aux_done, it["aux"] + 1)
                    slot = int(it["src"] == "y")
                    act.activation(rstd[:, slot], aux[:, 0:S + 2], ACT.Sqrt, bias=eps_col[0],
                                   scale=1.0 / D).then_inc(rooted, 1)
                elif kind == "tick":
                    if it["T"] and it["T"][0]["table"] != "decay":
                        unit, j = it["T"]
                        act.wait_ge(turned, unit["t"])
                        bank, dst = p_turned[unit["u"] % 2], four[:, 2 + unit["u"] % 2, :]
                        if unit["shape"] is FULL:
                            act.copy(dst, bank).then_inc(turned_read, 1)
                        else:
                            act.copy(dst[:, 0:S], bank[:, 0:S])
                            act.copy(dst[:, S + P:2 * S], bank[:, S + P:2 * S]).then_inc(turned_read, 1)
                    if it["S"] and it["S"][0]["table"] != "decay":
                        unit, comp, j = it["S"]
                        act.wait_ge(max_done, unit["max_n"][comp])
                        full = unit["shape"] is FULL
                        src = score[j % 2] if full else masked[:, j % 2, :]
                        for t, (at, width) in enumerate(unit["shape"]):
                            ins = act.activation(four[:, j % 2, at:at + width], src[:, at:at + width], ACT.Exp,
                                                 bias=small[:, j % 2, 2 + t:3 + t], scale=unit["scale"],
                                                 accum_out=small[:, j % 2, 4 + t:5 + t])
                        ins.then_inc(exp_done, 1)
                    if it["V"]:
                        unit, j = it["V"]
                        act.wait_ge(o_done, unit["u"] + 1)
                        r0, r1 = unit["out_row"], unit["out_row"] + unit["v_width"]
                        if unit["out"] == "obuf":
                            act.wait_ge(summed, it["stats"])
                            act.copy(obuf[:, unit["tile"]], o_bank[:, 0]).then_inc(o_copied, 1)
                        else:
                            n = unit["out_tiles"]
                            act.copy(mix_h[r0:r1, unit["tile"]:unit["tile"] + n], o_bank[r0:r1, 0:n]
                                     ).then_inc(o_hi, 1)
                elif kind == "pool":
                    act.wait_ge(chunk_used, it["acts_free"])
                    for kt in range(KT):
                        act.wait_ge(pooled, kt // 2 + 1)
                        act.copy(acts_h[:, kt], ybuf[:, kt]).then_inc(acts_hi, 1)
                elif kind == "head_norm":
                    pair = it["pair"]
                    act.wait_ge(o_copied, it["o_copied"])
                    act.wait_ge(mixed, it["mixed_before"])
                    act.wait_ge(summed, it["stats"])
                    act.activation(hn_sq, obuf[:, 2 * pair:2 * pair + 2], ACT.Square).then_inc(hn_squared, 1)
                    act.wait_ge(aux_done, it["aux"] + 1)
                    act.activation(hn_root.rearrange("p a b -> p (a b)"), aux[:], ACT.Sqrt,
                                   bias=eps_col[1 if it["which"] == "diff" else 0],
                                   scale=1.0 / P).then_inc(hn_rooted, 1)
                    for n in range(2):
                        act.wait_ge(hn_scaled, it["n"] + 1)
                        act.copy(mix_h[:, HN_TILE[it["which"]] + 2 * pair + n], hn_on[:, n]).then_inc(mix_hi, 1)
                elif kind == "gate_silu":
                    act.wait_ge(prod_read, it["e"])
                    act.activation(xq[:, it["at"]:it["at"] + 2], xq[:, it["at"]:it["at"] + 2],
                                   ACT.Silu).then_inc(gated, 1)
                elif kind == "lambda":
                    act.wait_ge(lam_part, 1)
                    act.activation(lam[:, 2:4], lam[:, 0:2], ACT.Exp).then_inc(lam_part, 1)

        @block.vector
        def _(dve):
            state = {"split": 0, "target": RING, "own": 0}

            def split(c, turn=0):
                if c >= N:
                    return
                dve.wait_ge(hi_done, turn * 6 + c + 1)
                dve.tensor_tensor(w_lo[:, c % RING], raw[:, c % RAW], w_hi[:, c % RING].bitcast(F32),
                                  ALU.subtract).then_inc(lo_done, 1)

            def flush(upto=None):
                upto = state["target"] if upto is None else upto
                while state["split"] < min(upto, N):
                    split(state["split"])
                    state["split"] += 1

            def own(ins):
                ins.then_inc(dve_step, 1)
                state["own"] += 1
                dve.wait_ge(dve_step, state["own"])

            def mid_low(it, i, turn):
                m = it["m"] + i
                dve.wait_ge(mid_hi, turn * 4 + m + 1)
                dve.tensor_tensor(mix_l[:, i % 4], four[:, 3, (m % 2) * S:(m % 2 + 1) * S],
                                  mix_h[:, i % 4].bitcast(F32), ALU.subtract).then_inc(mid_lo, 1)

            def ffn_part(it, p, turn, split_too=True):
                kind, i = ffn_step(p)
                c = it["c"] + p
                if kind == "up":
                    m = it["m"] + i
                    e = it["e"] + i
                    dve.wait_ge(chunk_used, turn * 6 + c + 1)
                    dve.tensor_tensor(four[:, m % 2, :].rearrange("p (a b) -> p a b", a=2), prod[e % 2][:],
                                      bcast(rstd[:, 0, 0:S], 2), ALU.mult).then_inc(prod_read, 1)
                    if i % 2:
                        mid_low(it, i - 1, turn)
                elif p < 32:
                    mid_low(it, 2 * i + 3, turn)
                if split_too:
                    split(c + RING - 1, turn)
                if kind == "up":
                    dve.wait_ge(silu_done, turn * 4 + m + 1)
                    dve.tensor_tensor(four[:, 3, (m % 2) * S:(m % 2 + 1) * S],
                                      four[:, 2, (m % 2) * S:(m % 2 + 1) * S], four[:, m % 2, S:2 * S],
                                      ALU.mult).then_inc(mid_done, 1)

            def reciprocal(it):
                slot = int(it["src"] == "y")
                dve.wait_ge(rooted, it["n"] + 1)
                own(dve.reciprocal(rstd[:, slot], rstd[:, slot]))

            def lo_tile(it, kt):
                dve.wait_ge(acts_hi, it["first"] + kt + 1)
                dve.scalar_tensor_tensor(out=acts_l[:, kt], in0=sources[it["src"]][:, kt],
                                         scalar=gain_col(it["gain"], kt), in1=acts_h[:, kt].bitcast(F32),
                                         op0=ALU.mult, op1=ALU.subtract).then_inc(acts_lo, 1)

            def wait_sum(it, b):
                if b < 3:
                    dve.wait_ge(acc_done, it["y"] - 3 + b + 1)
                else:
                    dve.wait_ge(chunk_used, it["y_chunk"])

            def add_pair(it, b, scale):
                wait_sum(it, b)
                dve.scalar_tensor_tensor(out=x[:, 2 * b:2 * b + 2], in0=acc[b][:], scalar=scale,
                                               in1=x[:, 2 * b:2 * b + 2], op0=ALU.mult, op1=ALU.add
                                         ).then_inc(x_new, 1)

            def tick(it):
                if it["F"]:
                    unit, comp, j = it["F"]
                    p = four[:, j % 2, :]
                    last = comp == unit["comps"] - 1
                    if unit["table"] == "decay":
                        dve.wait_ge(score_done, j + 1)
                        dve.wait_ge(o_done, unit["u"] - 1)
                        d = table("decay")[:, unit["head"] * S:(unit["head"] + 1) * S]
                        dve.tensor_tensor(p[:, 0:S], score[j % 2][:, 0:S], d, ALU.mult)
                        dve.tensor_tensor(p[:, S:S + P], score[j % 2][:, S:S + P], d[:, 0:P],
                                          ALU.mult).then_inc(decayed, 1)
                    else:
                        dve.wait_ge(exp_done, unit["max_n"][comp])
                        own(dve.reciprocal(small[:, j % 2, 6:8], small[:, j % 2, 4:6]))
                        if comp == 0:
                            for t, (at, width) in enumerate(unit["shape"]):
                                ins = dve.tensor_scalar(p[:, at:at + width], p[:, at:at + width],
                                                        small[:, j % 2, 6 + t:7 + t], None, ALU.mult)
                            if last:
                                ins.then_inc(weights_done, 1)
                            else:
                                own(ins)
                        else:
                            own(dve.tensor_scalar(small[:, j % 2, 6:8], small[:, j % 2, 6:8], lam[:, 8:9], None,
                                                  ALU.mult))
                            for t, (at, width) in enumerate(unit["shape"]):
                                ins = dve.scalar_tensor_tensor(
                                    out=p[:, at:at + width], in0=p[:, at:at + width],
                                    scalar=small[:, j % 2, 6 + t:7 + t], in1=four[:, (j - 1) % 2, at:at + width],
                                    op0=ALU.mult, op1=ALU.add)
                            ins.then_inc(weights_done, 1)
                if it["S"] and it["S"][0]["table"] != "decay":
                    unit, comp, j = it["S"]
                    dve.wait_ge(score_done, j + 1)
                    src = score[j % 2]
                    if unit["shape"] is not FULL:
                        slope = 1.0 if unit["slope"] is None else unit["slope"] / unit["scale"]
                        own(dve.scalar_tensor_tensor(out=masked[:, j % 2, :], in0=table(unit["table"]), scalar=slope,
                                                     in1=src[:, 0:384], op0=ALU.mult, op1=ALU.add))
                        src = masked[:, j % 2, :]
                    for t, (at, width) in enumerate(unit["shape"]):
                        ins = dve.tensor_reduce(small[:, j % 2, t:t + 1], src[:, at:at + width], AX.X, ALU.max,
                                                negate=True)
                    own(ins)
                    dve.tensor_scalar(small[:, j % 2, 2:4], small[:, j % 2, 0:2], unit["scale"], None,
                                      ALU.mult).then_inc(max_done, 1)
                if it["V"] and it["V"][0]["out"] == "mix":
                    unit, j = it["V"]
                    dve.wait_ge(o_hi, unit["o_hi"])
                    r0, r1 = unit["out_row"], unit["out_row"] + unit["v_width"]
                    for n in range(unit["out_tiles"]):
                        ins = dve.tensor_tensor(mix_l[r0:r1, unit["tile"] + n], o_bank[r0:r1, n],
                                                mix_h[r0:r1, unit["tile"] + n].bitcast(F32), ALU.subtract)
                        ins.then_inc(mixed, 1)

            dve.wait_ge(small_loaded, 64)
            own(dve.tensor_tensor(lam_prod(sq), lamb[:, :, 0], lamb[:, :, 1], ALU.mult))
            dve.tensor_reduce(lam[:, 0:2], lam_prod(sq), AX.X, ALU.add).then_inc(lam_part, 1)
            dve.wait_ge(lam_part, 2)
            own(dve.tensor_tensor(lam[:, 4:5], lam[:, 3:4], lam[:, 2:3], ALU.subtract))
            own(dve.tensor_scalar(lam[:, 8:9], lam[:, 4:5], -LAM_INIT, None, ALU.add))
            own(dve.tensor_scalar(lam[:, 9:10], vecs[:, DIFF_G:DIFF_G + 1], 1.0 - LAM_INIT, None, ALU.mult))
            flush()
            for it in items:
                kind = it["kind"]
                if kind == "ffn":
                    flush()
                    assert state["split"] == it["c"] + RING
                    for p in range(5):
                        ffn_part(it, p, 0, split_too=(p > 0))
                        if p == 1:
                            mid_low(it, 1, 0)
                    with dve.Fori(0, 4, 1) as turn:
                        for p in range(5, 11):
                            ffn_part(it, p, turn)
                    for p in range(29, 33):
                        ffn_part(it, p, 0, split_too=(p < 32))
                    state["split"] = it["c"] + 31 + RING
                    state["target"] = it["c"] + 33 + RING
                elif kind in ("cols", "rows_out", "down", "group"):
                    flush()
                    c = it["c"]
                    if kind == "cols":
                        e = it["e"]
                        dve.wait_ge(chunk_used, c + 1)
                        if it["dest"] == "u":
                            out = padded[:, it["at"]:it["at"] + 2, PAD:PAD + S]
                        else:
                            out = dests[it["dest"]][:, it["at"]:it["at"] + 2]
                        dve.tensor_tensor(out, prod[e % 2][:], bcast(rstd[:, 0, 0:S], 2),
                                          ALU.mult).then_inc(prod_read, 1)
                    elif kind == "rows_out":
                        e = it["e"]
                        dve.wait_ge(chunk_used, c + 1)
                        for t in range(2):
                            ins = dve.tensor_scalar(tok_dests[it["dest"]][:, t, it["at"]:it["at"] + COLS],
                                                    prod[e % 2][:, t], rstd[:, 0, S + t:S + t + 1], None, ALU.mult)
                        ins.then_inc(prod_read, 1)
                    elif kind == "group":
                        for g in range(4):
                            for half in range(2):
                                tile = 2 * g + half
                                dve.wait_ge(mix_hi, it["mix_hi"] + 2 * g + 2)
                                dve.scalar_tensor_tensor(
                                    out=mix_l[:, tile], in0=prod[(it["e"] + g) % 2][:, half],
                                    scalar=gain_col("pool_scale", tile), in1=mix_h[:, tile].bitcast(F32),
                                    op0=ALU.mult, op1=ALU.subtract).then_inc(mixed, 1)
                    state["target"] = c + 1 + RING
                elif kind == "prep":
                    if it["resid"] is not None:
                        flush(state["target"] - 1)
                        for b in range(4):
                            add_pair(it, b, it["resid"])
                            if b:
                                lo_tile(it, 2 * b - 2)
                                lo_tile(it, 2 * b - 1)
                        lo_tile(it, 6)
                        lo_tile(it, 7)
                    else:
                        for kt in range(KT):
                            lo_tile(it, kt)
                elif kind == "residual":
                    for b in range(4):
                        add_pair(it, b, it["scale"])
                elif kind == "post_norm_sums":
                    for b in range(4):
                        wait_sum(it, b)
                        dve.tensor_copy(ybuf[:, 2 * b:2 * b + 2], acc[b][:]).then_inc(y_copied, 1)
                elif kind == "stat":
                    dve.wait_ge(squared, it["n"] + 1)
                    dve.tensor_reduce(sums, sq[:].rearrange("p k t -> p t k"), AX.X,
                                      ALU.add).then_inc(summed, 1)
                    flush()
                    reciprocal(it)
                elif kind == "final_norm":
                    for kt in range(KT):
                        ins = dve.scalar_tensor_tensor(out=x[:, kt], in0=x[:, kt], scalar=gain_col(it["gain"], kt),
                                                       in1=rstd[:, 0, 0:S], op0=ALU.mult, op1=ALU.mult)
                        if kt % 2:
                            ins.then_inc(x_new, 1)
                elif kind == "post_norm":
                    for kt in range(KT):
                        ins = dve.scalar_tensor_tensor(out=ybuf[:, kt], in0=ybuf[:, kt],
                                                       scalar=gain_col(it["gain"], kt), in1=rstd[:, 1, 0:S],
                                                       op0=ALU.mult, op1=ALU.mult)
                    own(ins)
                    for b in range(4):
                        dve.tensor_tensor(x[:, 2 * b:2 * b + 2], x[:, 2 * b:2 * b + 2], ybuf[:, 2 * b:2 * b + 2],
                                          ALU.add).then_inc(x_new, 1)
                elif kind == "tick":
                    tick(it)
                elif kind == "rope":
                    dve.wait_ge(aux_done, it["aux"] + 1)
                    t = dests[it["dest"]][:, it["at"]:it["at"] + 2]
                    rot = sq[:, 6:8]
                    own(dve.tensor_tensor(rot, aux[:].rearrange("p (a b) -> p a b", a=2),
                                          bcast(table("sin_" + it["which"]), 2), ALU.mult))
                    own(dve.tensor_tensor(t, t, bcast(table("cos_" + it["which"]), 2), ALU.mult))
                    dve.tensor_tensor(t, t, rot, ALU.add).then_inc(roped, 1)
                elif kind == "pool":
                    for buf in shifted:
                        ins = dve.memset(buf[:, :, 0:PAD], 0.0)
                    own(dve.memset(padded[:, :, 0:PAD], 0.0))
                    for g in range(4):
                        u = padded[:, 2 * g:2 * g + 2]
                        src = u
                        for n in range(g + 1):
                            dst = shifted[n % 2]
                            own(dve.tensor_tensor(dst[:, :, PAD:], src[:, :, PAD:],
                                                  src[:, :, PAD - (1 << n):PAD + S - (1 << n)], ALU.add))
                            src = dst
                        w = 2 << g
                        out = ybuf[:, 2 * g:2 * g + 2]
                        dve.scalar_tensor_tensor(out=out, in0=src[:, :, PAD:], scalar=1.0 / w, in1=u[:, :, PAD:],
                                                 op0=ALU.mult, op1=ALU.subtract)
                        other = shifted[(g + 1) % 2]
                        own(dve.tensor_tensor(other[:, :, PAD:2 * PAD], src[:, :, PAD:2 * PAD],
                                              table("inv_count")[:, 16 * g:16 * g + 16].unsqueeze(1).broadcast_to(
                                                  [P, 2, 16]), ALU.mult))
                        dve.tensor_tensor(out[:, :, 0:16], other[:, :, PAD:2 * PAD], u[:, :, PAD:2 * PAD],
                                          ALU.subtract).then_inc(pooled, 1)
                        dve.wait_ge(pooled, g + 1)
                    for kt in range(KT):
                        dve.wait_ge(acts_hi, it["first"] + kt + 1)
                        dve.tensor_tensor(acts_l[:, kt], ybuf[:, kt], acts_h[:, kt].bitcast(F32),
                                          ALU.subtract).then_inc(acts_lo, 1)
                elif kind == "head_norm":
                    pair = it["pair"]
                    dve.wait_ge(hn_rooted, it["n"] + 1)
                    r = hn_root
                    own(dve.reciprocal(r, r))
                    src = obuf[:, 2 * pair:2 * pair + 2]
                    if it["which"] == "diff":
                        dve.scalar_tensor_tensor(out=hn_on, in0=src, scalar=lam[:, 9:10], in1=r, op0=ALU.mult,
                                                 op1=ALU.mult).then_inc(hn_scaled, 1)
                    else:
                        own(dve.tensor_tensor(hn_on, src, r, ALU.mult))
                        dve.wait_ge(gated, pair + 1)
                        dve.tensor_tensor(hn_on, hn_on, xq[:, 2 * pair:2 * pair + 2], ALU.mult
                                          ).then_inc(hn_scaled, 1)
                    for n in range(2):
                        tile = HN_TILE[it["which"]] + 2 * pair + n
                        dve.wait_ge(mix_hi, it["mix_hi"] + n + 1)
                        dve.tensor_tensor(mix_l[:, tile], hn_on[:, n], mix_h[:, tile].bitcast(F32),
                                          ALU.subtract).then_inc(mixed, 1)


def lam_prod(sq):
    return sq[:, 0, 0:128].rearrange("p (a b) -> p a b", a=2)


def number(plan):
    plan.score_reader, plan.o_reader = {}, {}
    aux_reader = None
    n = dict(decay=0, o_copied=0, rope=0, max=0, turned=0, o_hi=0, mix_hi=0, mixed=0, hn=0, stats=0, y_copied=0, mem=0)
    for it in plan.items:
        kind = it["kind"]
        if kind == "tick":
            if it["S"]:
                unit, comp, j = it["S"]
                if unit["table"] != "decay":
                    n["max"] += 1
                    unit.setdefault("max_n", {})[comp] = n["max"]
                    plan.score_reader[j] = ("exp_done", n["max"])
                else:
                    n["decay"] += 1
                    unit["d"] = n["decay"]
                    plan.score_reader[j] = ("decayed", n["decay"])
            if it["T"] and it["T"][0]["table"] != "decay":
                n["turned"] += 1
                it["T"][0]["t"] = n["turned"]
            if it["V"]:
                unit = it["V"][0]
                if unit["out"] == "mix":
                    n["o_hi"] += 1
                    unit["o_hi"] = n["o_hi"]
                    n["mixed"] += unit["out_tiles"]
                    plan.o_reader[unit["u"]] = ("mixed", n["mixed"])
                else:
                    it["stats"] = n["stats"]
                    n["o_copied"] += 1
                    plan.o_reader[unit["u"]] = ("o_copied", n["o_copied"])
        elif kind == "stat":
            it["hn"], it["mixed"] = n["hn"], n["mixed"]
            it["y_copied"] = n["y_copied"]
            n["stats"] += 1
            it["aux_reader"], aux_reader = aux_reader, ("rooted", n["stats"])
        elif kind == "rope":
            n["rope"] += 1
            it["aux_reader"], aux_reader = aux_reader, ("roped", n["rope"])
        elif kind == "post_norm_sums":
            n["y_copied"] += 4
        elif kind == "prep":
            if it["src"] == "mem":
                n["mem"] += 1
                it["mem_loaded"] = 16 if n["mem"] < 3 else 32
        elif kind == "group":
            it["mix_hi"], it["mixed"] = n["mix_hi"], n["mixed"]
            n["mix_hi"] += 8
            n["mixed"] += 8
        elif kind == "head_norm":
            it["mix_hi"], it["mixed_before"], it["stats"] = n["mix_hi"], n["mixed"], n["stats"]
            n["mix_hi"] += 2
            n["mixed"] += 2
            n["hn"] += 1
            it["o_copied"] = n["o_copied"]
            it["aux_reader"], aux_reader = aux_reader, ("hn_rooted", n["hn"])
        elif kind == "load_mem2":
            it["mixed"] = n["mixed"]
        if kind in ("down", "ffn"):
            it["t"] = n["turned"]
    assert n["mixed"] == plan.mixed


def kernel(**inputs):
    import concourse.bacc as bacc
    from concourse.bass_utils import run_bass_kernel_spmd

    inputs = {k: np.asarray(v) for k, v in inputs.items()}
    plan = make_plan()
    number(plan)
    weights = np.empty((plan.c, P, CHUNK), np.float32)
    for n, source in enumerate(plan.chunks):
        lay_out_chunk(inputs, source, weights[n])
    g = inputs["norm_g"]
    gains = {f"norm_g{i}{j}": g[i, j] for i in range(2) for j in range(3)}
    gains.update(mem_norm_g=inputs["mem_norm_g"], pool_scale=inputs["pool_scale"][0],
                 final_norm_g=inputs["final_norm_g"])
    for name in GAINS[9:]:
        gains[name] = inputs[name + "_2"][0]
    vecs = np.concatenate([columns(gains[name]) for name in GAINS] + [columns(inputs["diff_norm_g"][0])], 1)
    lam = np.ascontiguousarray(np.broadcast_to(inputs["diff_lambda"].reshape(1, 2, 2, 64), (P, 2, 2, 64)))
    arrays = {"x": features_first(inputs["x"]), "mem": features_first(inputs["mem"]),
              "mem2": features_first(inputs["mem_2"]), "weights": weights, "vecs": np.ascontiguousarray(vecs),
              "tabs": tables(), "lambda": lam}
    nc = bacc.Bacc("TRN2", target_bir_lowering=False, num_devices=1)
    A = {k: nc.dram_tensor(f"in_{k}_dram", a.shape, F32, kind="ExternalInput").ap() for k, a in arrays.items()}
    A["out"] = nc.dram_tensor("out_dram", (P, KT, S), F32, kind="ExternalOutput").ap()
    build(nc, A, plan)
    r = run_bass_kernel_spmd(nc, [{f"in_{k}_dram": a for k, a in arrays.items()}], core_ids=[0])
    out = r.results[0]["out_dram"]
    return np.ascontiguousarray(out.transpose(1, 0, 2).reshape(D, S).T)[None]
```

```python
import math
from contextlib import ExitStack

import numpy as np

import concourse.bass as bass
from concourse import mybir

F32 = mybir.dt.float32
F32R = mybir.dt.float32r
ALU = mybir.AluOpType
ACT = mybir.ActivationFunctionType
AX = mybir.AxisListType

P = 128
D = 1024
S = 256
KT = D // P
D_FF = 2816
MID_TILES = D_FF // P
CHUNK = 2048
POOL_WINDOWS = (2, 4, 8, 16)
RAW = 3
RING = 3
COLS = CHUNK // KT
DFF_STEPS = MID_TILES // 2
LAM_INIT = 0.8 - 0.6 * math.exp(-0.3 * 1)
HEADS = 8
CAUSAL = ((0, 128), (128, 256))
FULL = ((0, 256), (256, 256))

GAINS = ["norm_g00", "norm_g01", "norm_g02", "norm_g10", "norm_g11", "norm_g12", "mem_norm_g",
         "pool_scale", "final_norm_g", "g_pre_mix", "g_post_mix", "g_pre_cross", "g_mem",
         "g_post_cross", "g_pre_ffn", "g_post_ffn"]
GAIN = {name: KT * n for n, name in enumerate(GAINS)}
DIFF_G = KT * len(GAINS)
N_VECS = DIFF_G + 1
TABLES = {}
_at = 0
for _name, _width in (("ident", P), ("ones", P), ("perm_moba", P), ("perm_ret", P), ("alibi", 384),
                      ("mask", 384), ("cos_moba", S), ("sin_moba", S), ("cos_ret", S),
                      ("sin_ret", S), ("inv_count", 4 * 16), ("decay", 4 * S), ("eps", 2)):
    TABLES[_name] = (_at, _width)
    _at += _width
N_TABLES = _at


def tables():
    t = np.zeros((P, N_TABLES), np.float32)

    def put(name, a):
        at, width = TABLES[name]
        t[:, at:at + width] = a

    p = np.arange(P)
    put("ident", np.eye(P))
    put("ones", 1.0)
    k = np.arange(S)[None, :] - (P + p)[:, None]
    alibi = np.where(k <= 0, k, -1e30)
    mask = np.where(k <= 0, 0.0, -1e30)
    put("alibi", np.concatenate([alibi[:, P:], alibi], 1))
    put("mask", np.concatenate([mask[:, P:], mask], 1))
    pos = np.arange(S, dtype=np.float64)[None, :]
    for name, rot, inv in (
            ("moba", 16, 500000.0 ** (-np.arange(8) * 2.0 / 16)),
            ("ret", 64, 1.0 / 10000.0 ** np.linspace(0.0, 1.0, 32))):
        half = rot // 2
        perm = np.zeros((P, P))
        cos, sin = np.ones((P, S)), np.zeros((P, S))
        for base in (0, 64):
            for i in range(half):
                a, b = base + i, base + half + i
                perm[b, a] = -1.0
                perm[a, b] = 1.0
                for r in (a, b):
                    cos[r] = np.cos(pos * inv[i])
                    sin[r] = np.sin(pos * inv[i])
        put("perm_" + name, perm)
        put("cos_" + name, cos)
        put("sin_" + name, sin)
    inv_count = [1.0 / np.minimum(np.arange(1, 17), w) for w in POOL_WINDOWS]
    put("inv_count", np.concatenate(inv_count)[None, :])
    decay = []
    for h in range(4):
        lg = np.log(1.0 - 2.0 ** (-5.0 - h))
        d = np.arange(S)[None, :] - p[:, None]
        decay.append(np.where(d >= 0, np.exp(lg * np.maximum(d, 0)), 0.0) * 64 ** -0.5)
    put("decay", np.concatenate(decay, 1))
    put("eps", np.array([1e-6, 1e-5])[None, :])
    return t


class Plan:

    def __init__(self):
        self.items = []
        self.chunks = []
        self.c = self.e = self.m = self.y = self.j = self.u = self.aux = 0
        self.acts = 0
        self.x_new = 0
        self.mixed = 0
        self.tile_at = {}
        self.stat = 0
        self.rope_n = 0
        self.y_chunk = 0
        self.acc_taken = None
        self.y_copied = 0
        self.draining = False
        self.acc_j = 0
        self.open_steps = []
        self.late_steps = set()
        self.acts_users = 0
        self.hn = 0
        self.rg = 0

    def add(self, kind, **k):
        k["kind"] = kind
        self.items.append(k)
        return k

    def weights(self, keep=0):
        while len(self.open_steps) > keep:
            self.add("weights", F=self.open_steps.pop(0))

    def chunk(self, kind, source, **k):
        self.weights()
        self.chunks.append(source)
        item = self.add(kind, c=self.c, **k)
        self.c += 1
        if kind in ("cols", "rows_out"):
            self.acts_users = self.c
            item["e"] = self.e
            self.e += 1
        return item

    def statistic(self, src, after_chunk):
        self.add("stat", n=self.stat, src=src, aux=self.aux, after_chunk=after_chunk)
        self.stat += 1
        self.aux += 1

    def prep(self, src, gain, resid=None, after_chunk=True, squares=True):
        self.add("prep", src=src, gain=gain, resid=resid, first=self.acts, acts_free=self.acts_users,
                 x_new=self.x_new, y=self.y, y_chunk=self.y_chunk, n=self.stat, squares=squares)
        if resid is not None:
            self.x_new += 4
            if resid != "post":
                self.acc_taken = ("x_new", self.x_new)
        self.acts += KT
        if squares:
            self.statistic(src, after_chunk)

    def late_squares(self, src):
        self.add("late_squares", src=src, n=self.stat)
        self.statistic(src, True)

    def residual(self, scale):
        self.add("residual", scale=scale, y=self.y, y_chunk=self.y_chunk, x_new=self.x_new)
        self.x_new += 4
        self.acc_taken = ("x_new", self.x_new)

    def post_norm_sums(self, gain, after_chunk):
        self.add("post_norm_sums", y=self.y, y_chunk=self.y_chunk, gain=gain, n=self.stat,
                 y_copied=self.y_copied)
        self.y_copied += 4
        self.acc_taken = ("squared", 2 * self.stat + 2)
        self.statistic("y", after_chunk)

    def down(self, source_name, idx, pairs):
        for n, pair in enumerate(pairs):
            if n:
                yield
            self.chunk("down", (source_name, idx, "rows", pair), pair=pair, first=(n == 0),
                       last=(n == len(pairs) - 1), mixed=max(self.tile_at[2 * pair], self.tile_at[2 * pair + 1]),
                       j=self.acc_j, acc_taken=self.acc_taken)
        self.y += 3
        self.y_chunk = self.c

    def ffn(self, up, down, idx):
        item = self.add("ffn", c=self.c, e=self.e, m=self.m, y=self.y, acts=self.acts, acc_taken=self.acc_taken,
                        j=self.acc_j)
        for p in range(3 * DFF_STEPS):
            kind, i = ffn_step(p)
            self.chunks.append((up, idx, "gate_up", i) if kind == "up" else (down, idx, "rows", i))
        self.c += 3 * DFF_STEPS
        self.e += MID_TILES
        self.m += MID_TILES
        self.acts_users = self.c - 2
        self.y += 3
        self.y_chunk = self.c
        return item

    def project(self, source, col, dest, at, tokens_out=False, **k):
        return self.chunk("rows_out" if tokens_out else "cols", (*source, "cols", col), dest=dest,
                          at=at, acts=self.acts, **k)

    def ticks(self, units):
        subs = [(unit, comp) for unit in units for comp in range(unit["comps"])]
        made, transposed = [], None
        while subs or any(made[-2:]) or transposed:
            open_s = bool(subs) and subs[0][0]["need"] is not None and (
                self.draining or self.c >= subs[0][0]["ready_c"])
            pending = any(made[-2:]) or transposed
            if not open_s and not pending or (transposed and transposed[0]["need_v"] is None):
                yield "blocked"
                continue
            tick = {"S": None, "T": None, "V": transposed}
            new = None
            if open_s:
                unit, comp = subs.pop(0)
                if comp == 0:
                    unit["u"] = self.u
                    self.u += 1
                new = tick["S"] = (unit, comp, self.j)
                if self.draining:
                    self.late_steps.add(self.j)
                    tick["e"] = self.e
                else:
                    tick["acc_taken"] = self.acc_taken
                    self.acc_j = self.j + 1
                self.j += 1
            if len(made) >= 2 and made[-2]:
                unit, comp, j = made[-2]
                if comp == unit["comps"] - 1:
                    tick["T"] = (unit, j)
                    unit["late"] = self.draining
            made.append(new)
            if transposed:
                unit = transposed[0]
                unit["is_out"] = True
                if unit["out"] == "mix":
                    for n in range(unit["out_tiles"]):
                        self.mixed += 1
                        self.tile_at[unit["tile"] + n] = self.mixed
            transposed = tick["T"]
            if new:
                self.add("tick", **tick)
                self.open_steps.append(new)
                self.weights(keep=1)
            else:
                self.weights()
                self.add("tick", **tick)
            yield

    def ready(self, units, delay=1):
        for unit in units:
            unit["need"], unit["ready_c"], unit["rope"] = self.e, self.c + delay, self.rope_n

    def ready_v(self, units):
        for unit in units:
            unit["need_v"] = self.e

    def head_squares(self, pair, which):
        self.add("head_squares", pair=pair, which=which)

    def head_norm(self, pair, which):
        self.add("head_norm", pair=pair, which=which, n=self.hn, aux=self.aux)
        self.hn += 1
        self.aux += 1

    def head_split(self, pair, which):
        self.add("head_split", pair=pair, which=which, n=self.hn - 1)
        for n in range(2):
            self.mixed += 1
            self.tile_at[HN_TILE[which] + 2 * pair + n] = self.mixed

    def final_prep(self):
        self.add("prep", src="x", gain="both", resid=0.5, first=self.acts, acts_free=self.acts_users,
                 x_new=self.x_new, y=self.y, y_chunk=self.y_chunk, n=self.stat, double=True, squares=True)
        self.x_new += 4
        self.acc_taken = ("x_new", self.x_new)
        self.acts += KT
        self.statistic("x", True)
        self.add("final_squares", n=self.stat)
        self.statistic("z", True)

    def rope(self, dest, at, which, e):
        self.add("rope", dest=dest, at=at, which=which, e=e, aux=self.aux)
        self.aux += 1
        self.rope_n += 1


HN_TILE = {"diff": 0, "ret": 4}


def ffn_step(p):
    if p < 2:
        return "up", p
    i, r = 1 + (p - 2) // 3, (p - 2) % 3
    if i == DFF_STEPS:
        return "down", DFF_STEPS - 1
    return ("up", 2 * i + r) if r < 2 else ("down", i - 1)


def interleave(ticks, n):
    for _ in range(n):
        if next(ticks, "end") is not None:
            return


def unit_of(head, **k):
    return dict(dict(head=head, comps=1, slope=None, tiles=1, v_width=P, out_tiles=1, out_row=0,
                     tile=head, need=None, need_v=None, is_out=False), **k)


def mem_units(heads, dims, q):
    tiles = dims // P
    return [unit_of(h, shape=FULL, table=None, scale=dims ** -0.5, q=(q, h * tiles), k=("mem_k", h * tiles),
                    rows=(0, P), tiles=tiles, v=("mem_v", h * dims), out="mix", out_tiles=tiles,
                    tile=(8 if tiles == 1 else 0) + h * tiles) for h in range(heads)]


class HeadNorms:

    def __init__(self, pl, units, which):
        self.pl, self.units, self.which = pl, units, which
        self.squared = self.normed = self.split = 0

    def step(self):
        if self.squared > self.normed:
            self.pl.head_norm(self.normed, self.which)
            self.normed += 1
            return
        if self.normed > self.split:
            self.pl.head_split(self.split, self.which)
            self.split += 1
        if 2 * self.squared < len(self.units) and all(
                u["is_out"] for u in self.units[2 * self.squared:2 * self.squared + 2]):
            self.pl.head_squares(self.squared, self.which)
            self.squared += 1

    def finished(self):
        return 2 * self.split == len(self.units)


def make_plan():
    pl = Plan()

    def kv(layer):
        for n in range(2):
            pl.project(("mem_w_kv", layer), n * COLS, "mem_k", 2 * n)
        for n in range(2):
            pl.project(("mem_w_kv", layer), 512 + n * COLS, "mem_v", n * COLS, tokens_out=True)

    def drain(*steps):
        pl.draining = True
        for step in steps:
            assert step() != "blocked"
        pl.draining = False

    def stepper(generator):
        return lambda: next(generator, None)

    pl.prep("x", "norm_g00")
    pl.ffn("ffn_w_up", "ffn_w_down", (0, 0))
    pl.add("lambda")
    pl.prep("mem", "mem_norm_g")
    pl.residual(0.5)
    kv(0)
    pl.prep("x", "norm_g01")
    for n in range(2):
        pl.project(("pool_w_in", 0), D + n * COLS, "xq", 2 * n)
    units = mem_units(4, P, "xq")
    pl.ready(units)
    pl.ready_v(units)
    ticks = pl.ticks(units)
    for g in (3, 2, 1, 0):
        pl.project(("pool_w_in", 0), g * COLS, "u", 2 * g)
        interleave(ticks, 2)
        pl.weights()
        pl.add("pool", g=g, e=pl.e)
    pl.draining = True
    while next(ticks, "end") != "end":
        pass
    pl.draining = False
    pl.add("pool_split", first=pl.acts, acts_free=pl.acts_users)
    pl.acts += KT

    def pool_down(pair, **k):
        pl.chunk("down", ("pool_w_out", 0, "rows", pair), pair=pair,
                 mixed=max(pl.tile_at[2 * pair], pl.tile_at[2 * pair + 1]), j=pl.acc_j,
                 acc_taken=pl.acc_taken, **k)

    pool_down(4, first=True, last=False)
    pool_down(5, first=False, last=False)
    pl.chunk("group", ("pool_w_group", 0, "group", 0), e=pl.e, acts=pl.acts)
    for t in range(8):
        pl.mixed += 1
        pl.tile_at[t] = pl.mixed
    for pair in range(4):
        pool_down(pair, first=False, last=(pair == 3))
    pl.y += 3
    pl.y_chunk = pl.c
    pl.prep("x", "norm_g02", resid=1.0)
    pl.ffn("ffn_w_up", "ffn_w_down", (0, 1))
    pl.prep("x", "norm_g10", resid=0.5)
    pl.ffn("ffn_w_up", "ffn_w_down", (1, 0))
    pl.prep("mem", "mem_norm_g")
    pl.residual(0.5)
    kv(1)
    pl.prep("x", "norm_g11")
    w = ("diff_w_in", 0)
    for n in range(2):
        pl.project(w, 3 * D + n * COLS, "xq", 2 * n)
    memory = mem_units(4, P, "xq")
    pl.ready(memory)
    pl.ready_v(memory)
    slopes = [2.0 ** (-8.0 * (h + 1) / HEADS) for h in range(HEADS)]
    heads = [unit_of(h, comps=2, shape=CAUSAL, table="alibi", slope=slopes[h], scale=64 ** -0.5, q=("q", h),
                     k=("k", h), rows=None, v=("v", h * P), out="obuf") for h in range(HEADS)]
    ticks = pl.ticks(memory + heads)
    norms = HeadNorms(pl, heads, "diff")
    for name, pair in (("q", 0), ("k", 0), ("q", 1), ("v", 0), ("k", 1), ("q", 2), ("k", 2), ("v", 1),
                       ("q", 3), ("k", 3), ("v", 2), ("v", 3)):
        col = {"q": 0, "k": D, "v": 2 * D}[name] + pair * COLS
        mine = heads[2 * pair:2 * pair + 2]
        if name == "v":
            pl.project(w, col, "v", pair * COLS, tokens_out=True)
            pl.ready_v(mine)
        else:
            pl.project(w, col, name, 2 * pair)
            if name == "k":
                pl.ready(mine)
        if pair < 3 or name != "v":
            interleave(ticks, 2)
            norms.step()
    tick, down = stepper(ticks), stepper(pl.down("diff_w_out", 0, [4, 5, 0, 1, 2, 3]))
    drain(tick, norms.step, down, tick, tick, norms.step, down, tick, norms.step, down, tick, norms.step,
          down, norms.step, down, norms.step, down)
    assert norms.finished()
    pl.prep("x", "norm_g12", resid=1.0)
    pl.ffn("ffn_w_up", "ffn_w_down", (1, 1))
    pl.final_prep()
    w = ("w_in_2", 0)
    moba = [unit_of(h, shape=CAUSAL, table="mask", scale=64 ** -0.5, q=("q", h // 2), k=("k", h // 2),
                    rows=(64 * (h % 2), 64 * (h % 2) + 64), v=("v", 64 * h), v_width=64, out="mix",
                    tile=h // 2, out_row=64 * (h % 2)) for h in range(8)]
    ret = [unit_of(h, shape=CAUSAL, table="decay", scale=1.0, q=("k", 4 + h // 2), k=("k", 6 + h // 2),
                   rows=(64 * (h % 2), 64 * (h % 2) + 64), v=("v", 512 + h * P), out="obuf") for h in range(4)]
    ticks = pl.ticks(moba[0:4] + ret + moba[4:8])
    norms = HeadNorms(pl, ret, "ret")
    pl.project(w, 0, "q", 0)
    pl.project(w, 512, "k", 0)
    pl.rope("q", 0, "moba", pl.e - 1)
    pl.add("x_final", x_new=pl.x_new)
    pl.x_new += 4
    pl.project(w, 1536, "k", 4)
    pl.rope("k", 0, "moba", pl.e - 1)
    pl.ready(moba[0:4])
    pl.project(w, 1792, "k", 6)
    pl.rope("k", 4, "ret", pl.e - 1)
    pl.project(w, 1024, "v", 0, tokens_out=True)
    pl.ready_v(moba[0:4])
    pl.rope("k", 6, "ret", pl.e - 1)
    pl.ready(ret)
    interleave(ticks, 2)
    for n in range(2):
        pl.project(w, 2048 + n * COLS, "v", 512 + n * COLS, tokens_out=True)
        if n:
            pl.ready_v(ret)
        interleave(ticks, 2)
    pl.project(w, 2560, "rg", 0)
    interleave(ticks, 2)
    pl.project(w, 2560 + COLS, "rg", 2)
    pl.add("gate_silu", e=pl.e - 1, at=0)
    interleave(ticks, 2)
    norms.step()
    pl.project(w, COLS, "q", 2)
    pl.add("gate_silu", e=pl.e - 1, at=2)
    interleave(ticks, 2)
    norms.step()
    pl.project(w, 512 + COLS, "k", 2)
    pl.rope("q", 2, "moba", pl.e - 1)
    interleave(ticks, 2)
    norms.step()
    pl.project(w, 1024 + COLS, "v", COLS, tokens_out=True)
    pl.ready_v(moba[4:8])
    pl.rope("k", 2, "moba", pl.e - 1)
    pl.ready(moba[4:8], delay=0)
    tick, down = stepper(ticks), stepper(pl.down("w_out_2", 0, [2, 0, 3, 1]))
    drain(down, norms.step, tick, tick, down, norms.step)
    assert norms.finished()
    pl.add("load_mem2")
    drain(tick, tick, down, tick, tick, tick)
    pl.prep("mem", "g_mem", squares=False)
    pl.late_squares("mem")
    down()
    pl.post_norm_sums("g_post_mix", after_chunk=True)
    for n in range(4):
        pl.project(("w_ckv_2", 0), n * COLS, "mem_k", 2 * n)
        if n == 1:
            pl.add("post_norm", x_new=pl.x_new)
            pl.x_new += 4
    for n in range(4):
        pl.project(("w_ckv_2", 0), D + n * COLS, "mem_v", n * COLS, tokens_out=True)
    pl.prep("x", "g_pre_cross")
    units = mem_units(4, 2 * P, "q")
    ticks = pl.ticks(units)
    for n in range(4):
        pl.project(("w_cq_2", 0), n * COLS, "q", 2 * n)
        pl.ready(units[n:n + 1])
        pl.ready_v(units[n:n + 1])
        if n < 3:
            interleave(ticks, 1)
    tick, down = stepper(ticks), stepper(pl.down("w_co_2", 0, [0, 1, 2, 3]))
    drain(tick, tick, tick, down, tick, down, tick, down, down)
    pl.post_norm_sums("g_post_cross", after_chunk=False)
    pl.prep("x", "g_pre_ffn", resid="post")
    pl.ffn("w_gate_up_2", "w_down_2", 0)
    pl.post_norm_sums("g_post_ffn", after_chunk=False)
    pl.add("post_norm", x_new=pl.x_new)
    pl.add("store", x_new=pl.x_new)
    pl.x_new += 4
    return pl


def columns(a):
    return np.asarray(a).reshape(-1, P).T


def features_first(a):
    return np.ascontiguousarray(np.asarray(a)[0].T.reshape(KT, P, S).transpose(1, 0, 2))


def lay_out_chunk(inputs, source, out):
    name, idx, how, at = source
    w = inputs[name][idx]
    if how == "gate_up":
        v = w.reshape(KT, P, 2, D_FF)[:, :, :, at * P:(at + 1) * P].transpose(1, 0, 2, 3)
        out.reshape(P, KT, 2, P)[...] = v
    elif how == "cols":
        v = w.reshape(KT, P, -1)[:, :, at:at + COLS].transpose(1, 0, 2)
        out.reshape(P, KT, COLS)[...] = v
    elif how == "rows":
        v = w[2 * P * at:2 * P * (at + 1)].reshape(2, P, D).transpose(1, 0, 2)
        out.reshape(P, 2, D)[...] = v
    else:
        out.reshape(P, 8, COLS)[...] = w.reshape(8, P, COLS).transpose(1, 0, 2)


def build(nc, A, plan):
    items = plan.items
    N = plan.c
    assert len(plan.chunks) == N

    with ExitStack() as ctx:
        def sb(name, shape, dt=F32):
            return ctx.enter_context(nc.sbuf_tensor(name, shape, dt))

        def sem(name):
            return ctx.enter_context(nc.semaphore(name))

        raw = sb("raw", [P, RAW, CHUNK])
        w_hi = sb("w_hi", [P, RING, CHUNK], F32R)
        w_lo = sb("w_lo", [P, RING, CHUNK], F32R)
        x = sb("x_res", [P, KT, S])
        acts_h = sb("acts_h", [P, KT, S], F32R)
        acts_l = sb("acts_l", [P, KT, S], F32R)
        mix_h = sb("mix_h", [P, 12, S], F32R)
        mix_l = sb("mix_l", [P, 12, S], F32R)
        mem_k = sb("mem_k", [P, KT, S])
        mem_v = sb("mem_v", [P, 2, D])
        work = sb("work", [P, 3 * KT * S])
        xq = sb("xq", [P, 4, S])
        mem_x = sb("mem_x", [P, KT, S])
        sq = sb("sq", [P, KT, S])
        four = sb("four", [P, 4, 512])
        masked = sb("masked", [P, 2, 384])
        rstd = sb("rstd", [P, 2, S + 2])
        small = sb("small", [P, 3, 8])
        lam = sb("lam", [P, 12])
        vecs = sb("vecs", [P, N_VECS])
        both_g = sb("both_g", [P, KT])
        tabs = sb("tabs", [P, N_TABLES])

        q_t = work[:, 0:KT * S].rearrange("p (k t) -> p k t", t=S)
        k_t = work[:, KT * S:2 * KT * S].rearrange("p (k t) -> p k t", t=S)
        v_flat = work[:, 2 * KT * S:3 * KT * S]
        v_t = v_flat.rearrange("p (t n) -> p t n", t=2)
        ybuf = v_flat.rearrange("p (k t) -> p k t", t=S)
        PAD = 16
        padded = work[:, 0:KT * (S + PAD)].rearrange("p (k t) -> p k t", t=S + PAD)
        shifted = [work[:, 2176 + 544 * n:2176 + 544 * (n + 1)].rearrange("p (k t) -> p k t", t=S + PAD)
                   for n in range(2)]
        obuf = mem_x
        dests = {"q": q_t, "k": k_t, "xq": xq[:], "rg": xq[:], "mem_k": mem_k[:]}
        tok_dests = {"v": v_t, "mem_v": mem_v[:]}
        sources = {"x": x[:], "mem": mem_x[:], "y": ybuf}
        hn_sq = sq[:, 0:2, :]
        hn_root = hn_sq
        hn_on = sq[:, 2:4, :]
        rotated = sq[:, 4:6, :]
        p_slots = [four[:, 0, :], four[:, 1, :], sq[:, 6:8, :].rearrange("p a b -> p (a b)")]
        pt_slots = [four[:, 2, :], four[:, 3, :]]
        sums = four[:, 0, :].rearrange("p (a b) -> p a b", a=2)
        lamb = masked[:, 0, 0:256].rearrange("p (a b c) -> p a b c", a=2, b=2)
        lam_prod = masked[:, 1, 0:128].rearrange("p (a b) -> p a b", a=2)

        def table(name):
            at, width = TABLES[name]
            return tabs[:, at:at + width]

        def gain_col(name, kt):
            if name == "both":
                return both_g[:, kt:kt + 1]
            at = GAIN[name] + kt
            return vecs[:, at:at + 1]

        eps_col = {0: table("eps")[:, 0:1], 1: table("eps")[:, 1:2]}
        ident, ones = table("ident"), table("ones")

        acc = [ctx.enter_context(nc.psum_tensor(f"acc{b}", [P, 2, S], F32)) for b in range(4)]
        prod = [ctx.enter_context(nc.psum_tensor(f"prod{b}", [P, 2, S], F32)) for b in range(2)]
        aux = ctx.enter_context(nc.psum_tensor("aux", [P, 512], F32))
        o_bank = ctx.enter_context(nc.psum_tensor("o_bank", [P, 2, S], F32))
        score = [acc[b][:].rearrange("p a b -> p (a b)") for b in (0, 1)]
        p_turned = [acc[b][:].rearrange("p a b -> p (a b)") for b in (2, 3)]

        raw_loaded = [sem(f"raw_loaded{n}") for n in range(RAW)]
        vecs_loaded = sem("vecs_loaded")
        x_loaded = [sem(f"x_loaded{n}") for n in range(2)]
        tabs_loaded = sem("tabs_loaded")
        lam_loaded = sem("lam_loaded")
        mem_loaded = sem("mem_loaded")
        hi_done = sem("hi_done")
        lo_done = sem("lo_done")
        chunk_used = sem("chunk_used")
        group_done = sem("group_done")
        prod_read = sem("prod_read")
        silu_done = sem("silu_done")
        mid_done = sem("mid_done")
        mid_hi = sem("mid_hi")
        mid_lo = sem("mid_lo")
        acc_done = sem("acc_done")
        x_new = sem("x_new")
        acts_hi = sem("acts_hi")
        acts_lo = sem("acts_lo")
        y_copied = sem("y_copied")
        squared = sem("squared")
        summed = sem("summed")
        aux_done = sem("aux_done")
        scaled_ms = sem("scaled_ms")
        rooted = sem("rooted")
        score_done = sem("score_done")
        decayed = sem("decayed")
        max_done = sem("max_done")
        exp_done = sem("exp_done")
        weights_done = sem("weights_done")
        turned = sem("turned")
        turned_read = sem("turned_read")
        o_done = sem("o_done")
        o_hi = sem("o_hi")
        o_copied = sem("o_copied")
        mix_hi = sem("mix_hi")
        mixed = sem("mixed")
        hn_squared = sem("hn_squared")
        hn_rooted = sem("hn_rooted")
        hn_scaled = sem("hn_scaled")
        roped = sem("roped")
        pooled = sem("pooled")
        gated = sem("gated")
        lam_part = sem("lam_part")
        act_step = sem("act_step")
        dve_step = sem("dve_step")
        stored = sem("stored")

        by_name = {"x_new": x_new, "y_copied": y_copied, "exp_done": exp_done, "decayed": decayed,
                   "rooted": rooted, "hn_rooted": hn_rooted, "roped": roped, "mixed": mixed,
                   "o_copied": o_copied, "squared": squared, "turned_read": turned_read}

        def score_at(j):
            if j in plan.late_steps:
                return prod[j % 2][:].rearrange("p a b -> p (a b)")
            return score[j % 2]

        def turned_at(unit):
            return aux[:] if unit["late"] else p_turned[unit["u"] % 2]

        def reader(engine, told):
            if told:
                engine.wait_ge(by_name[told[0]], told[1])

        block = ctx.enter_context(nc.Block())

        def bcast(ap, n):
            return ap.unsqueeze(1).broadcast_to([P, n, S])

        @block.sync
        def _(sp):
            weights = A["weights"]
            sp.dma_start(vecs[:], A["vecs"]).then_inc(vecs_loaded, 16)
            sp.dma_start(x[:, 0:4], A["x"][:, 0:4]).then_inc(x_loaded[0], 16)
            sp.dma_start(raw[:, 0], weights[0]).then_inc(raw_loaded[0], 16)
            sp.dma_start(x[:, 4:8], A["x"][:, 4:8]).then_inc(x_loaded[1], 16)
            sp.dma_start(raw[:, 1], weights[1]).then_inc(raw_loaded[1], 16)
            sp.dma_start(tabs[:], A["tabs"]).then_inc(tabs_loaded, 16)
            sp.dma_start(raw[:, 2], weights[2]).then_inc(raw_loaded[2], 16)
            turns = (N - RAW) // RAW
            with sp.Fori(0, turns, 1) as i:
                for n in range(RAW):
                    sp.wait_ge(lo_done, i * RAW + n + 1)
                    sp.dma_start(raw[:, n], weights[bass.ds(i * RAW + n + RAW, 1)].rearrange("o p f -> (o p) f")
                                 ).then_inc(raw_loaded[n], 16)
            for c in range(RAW * (turns + 1), N):
                sp.wait_ge(lo_done, c - RAW + 1)
                sp.dma_start(raw[:, c % RAW], weights[c]).then_inc(raw_loaded[c % RAW], 16)
            first = items[-1]["x_new"]
            for b in range(4):
                sp.wait_ge(x_new, first + b + 1)
                sp.dma_start(A["out"][:, 2 * b:2 * b + 2], x[:, 2 * b:2 * b + 2]).then_inc(stored, 16)
            sp.wait_ge(stored, 64)

        @block.gpsimd
        def _(pool):
            pool.wait_ge(chunk_used, 3)
            pool.dma_start(lamb, A["lambda"]).then_inc(lam_loaded, 16)
            pool.dma_start(mem_x[:], A["mem"]).then_inc(mem_loaded, 16)
            for it in items:
                if it["kind"] == "load_mem2":
                    pool.wait_ge(mixed, it["mixed"])
                    pool.dma_start(mem_x[:], A["mem2"]).then_inc(mem_loaded, 16)

        @block.tensor
        def _(pe):
            seen = {"acts": 0}

            def passes(out, w, moving_hi, moving_lo, slot, first, last):
                pe.matmul(out, w(w_hi, slot), moving_hi, start=first, stop=False, skip_group_check=True)
                pe.matmul(out, w(w_hi, slot), moving_lo, start=False, stop=False, skip_group_check=True)
                return pe.matmul(out, w(w_lo, slot), moving_hi, start=False, stop=last, skip_group_check=True)

            def columns_chunk(slot, bank, acts):
                for kt in range(KT):
                    if acts is not None and seen["acts"] < acts:
                        pe.wait_ge(acts_lo, acts - KT + kt + 1)
                    for half in range(2):
                        mm = passes(prod[bank][:, half],
                                    lambda w, s, a=kt * COLS + half * P: w[:, s, a:a + P],
                                    acts_h[:, kt], acts_l[:, kt], slot, kt == 0 and half == 0, kt == KT - 1)
                if acts is not None:
                    seen["acts"] = max(seen["acts"], acts)
                return mm

            def tokens_chunk(slot, bank, acts):
                if seen["acts"] < acts:
                    pe.wait_ge(acts_lo, acts)
                    seen["acts"] = acts
                for t in range(2):
                    for kt in range(KT):
                        a_h = acts_h[:, kt, t * P:(t + 1) * P]
                        a_l = acts_l[:, kt, t * P:(t + 1) * P]
                        wh = w_hi[:, slot, kt * COLS:(kt + 1) * COLS]
                        wl = w_lo[:, slot, kt * COLS:(kt + 1) * COLS]
                        out = prod[bank][:, t]
                        pe.matmul(out, a_h, wh, start=(kt == 0), stop=False, skip_group_check=True)
                        pe.matmul(out, a_h, wl, start=False, stop=False, skip_group_check=True)
                        mm = pe.matmul(out, a_l, wh, start=False, stop=(kt == KT - 1), skip_group_check=True)
                return mm

            def down_chunk(slot, tiles, first, last):
                for b in range(4):
                    for n, tile in enumerate(tiles):
                        for half in range(2):
                            a = n * D + (2 * b + half) * P
                            mm = passes(acc[b][:, half], lambda w, s, a=a: w[:, s, a:a + P], mix_h[:, tile],
                                        mix_l[:, tile], slot, first and n == 0 and half == 0, last and n == 1)
                    if last and b < 3:
                        mm.then_inc(acc_done, 1)
                mm.then_inc(chunk_used, 1)

            def statistic(it):
                pe.wait_ge(summed, 2 * it["n"] + 2)
                if it["n"] == 0:
                    pe.wait_ge(tabs_loaded, 16)
                reader(pe, it["aux_reader"])
                for h in range(2):
                    pe.matmul(aux[:, 0:S], ones, sums[:, h], start=(h == 0), stop=(h == 1))
                for t in range(2):
                    for h in range(2):
                        mm = pe.matmul(aux[:, S + t:S + t + 1], sums[:, h, t * P:(t + 1) * P], ones[:, 0:1],
                                       start=(h == 0), stop=(h == 1))
                mm.then_inc(aux_done, 1)

            def ffn_part(it, p, turn):
                kind, i = ffn_step(p)
                c = it["c"] + p
                pe.wait_ge(lo_done, turn * 6 + c + 1)
                if kind == "up":
                    e = it["e"] + i
                    if e >= 2:
                        pe.wait_ge(prod_read, turn * 4 + e - 1)
                    columns_chunk(c % RING, e % 2, it["acts"]).then_inc(chunk_used, 1)
                else:
                    pe.wait_ge(mid_lo, turn * 4 + it["m"] + 2 * i + 2)
                    if i == 0:
                        free_accumulators(it)
                    down_chunk(c % RING, [(2 * i) % 4, (2 * i + 1) % 4], i == 0, i == DFF_STEPS - 1)

            def free_accumulators(it):
                reader(pe, it["acc_taken"])
                for j in (it["j"] - 2, it["j"] - 1):
                    reader(pe, plan.score_reader.get(j))
                if it["t"]:
                    pe.wait_ge(turned_read, it["t"])

            def tick(it):
                if it["S"]:
                    unit, comp, j = it["S"]
                    pe.wait_ge(prod_read, unit["need"])
                    if unit["rope"]:
                        pe.wait_ge(roped, unit["rope"])
                    if j in plan.late_steps:
                        pe.wait_ge(prod_read, it["e"])
                    else:
                        reader(pe, it["acc_taken"])
                    reader(pe, plan.score_reader.get(j - 2))
                    r0, r1 = unit["rows"] or (64 * comp, 64 * comp + 64)
                    q, qt = unit["q"]
                    k, kt = unit["k"]
                    bank = score_at(j)
                    if unit["table"] == "decay":
                        for t, (at, width) in enumerate(((0, 256), (256, 128))):
                            mm = pe.matmul(bank[:, at:at + width], dests[k][r0:r1, kt, t * P:(t + 1) * P],
                                           dests[q][r0:r1, qt, S - width:S], start=True, stop=True)
                    else:
                        for t, (at, width) in enumerate(unit["shape"]):
                            for n in range(unit["tiles"]):
                                mm = pe.matmul(bank[:, at:at + width],
                                               dests[q][r0:r1, qt + n, t * P:(t + 1) * P],
                                               dests[k][r0:r1, kt + n, 0:width], start=(n == 0),
                                               stop=(n == unit["tiles"] - 1))
                    mm.then_inc(score_done, 1)
                if it["T"] and it["T"][0]["table"] != "decay":
                    unit, j = it["T"]
                    pe.wait_ge(weights_done, unit["t"])
                    bank = turned_at(unit)
                    if unit["late"]:
                        reader(pe, it["aux_reader"])
                    for t, (at, width) in enumerate(unit["shape"]):
                        for m in range(width // P):
                            mm = pe.transpose(bank[:, m * S + t * P:m * S + (t + 1) * P],
                                              p_slots[j % 3][:, at + m * P:at + (m + 1) * P], ident)
                    mm.then_inc(turned, 1)
                if it["V"]:
                    unit, j = it["V"]
                    v, col = unit["v"]
                    vt = tok_dests[v]
                    w = unit["v_width"]
                    pe.wait_ge(prod_read, unit["need_v"])
                    decay = unit["table"] == "decay"
                    if decay:
                        pe.wait_ge(decayed, unit["d"])
                    else:
                        pe.wait_ge(turned_read, unit["t"])
                    reader(pe, plan.o_reader.get(unit["u"] - 1))
                    for n in range(unit["out_tiles"]):
                        c = col + n * P
                        out = o_bank[unit["out_row"]:unit["out_row"] + w, n]
                        if unit["shape"] is FULL:
                            src = pt_slots[unit["u"] % 2]
                            pe.matmul(out, vt[:, 0, c:c + w], src[:, 0:S], start=True, stop=False)
                            mm = pe.matmul(out, vt[:, 1, c:c + w], src[:, S:2 * S], start=False, stop=True)
                        else:
                            src = p_slots[j % 3] if decay else pt_slots[unit["u"] % 2]
                            late = src[:, S:S + P] if decay else src[:, S + P:2 * S]
                            pe.matmul(out, vt[:, 0, c:c + w], src[:, 0:S], start=True, stop=False,
                                      skip_group_check=True)
                            mm = pe.matmul(out[:, P:S], vt[:, 1, c:c + w], late, start=False, stop=True,
                                           skip_group_check=True)
                    mm.then_inc(o_done, 1)

            late_statistics = []
            for it in items:
                kind = it["kind"]
                if kind == "ffn":
                    for told in it["late_readers"]:
                        reader(pe, told)
                    for p in range(5):
                        ffn_part(it, p, 0)
                        if p == 0 and late_statistics:
                            statistic(late_statistics.pop(0))
                    with pe.Fori(0, 4, 1) as turn:
                        for p in range(5, 11):
                            ffn_part(it, p, turn)
                    for p in range(29, 33):
                        ffn_part(it, p, 0)
                elif kind in ("cols", "rows_out", "down", "group"):
                    c = it["c"]
                    pe.wait_ge(lo_done, c + 1)
                    for told in it["late_readers"]:
                        reader(pe, told)
                    if kind in ("cols", "rows_out"):
                        if it["e"] >= 2:
                            pe.wait_ge(prod_read, it["e"] - 1)
                        part = columns_chunk if kind == "cols" else tokens_chunk
                        part(c % RING, it["e"] % 2, it["acts"]).then_inc(chunk_used, 1)
                    elif kind == "down":
                        pe.wait_ge(mixed, it["mixed"])
                        if it["first"]:
                            free_accumulators(it)
                        down_chunk(c % RING, [2 * it["pair"], 2 * it["pair"] + 1], it["first"], it["last"])
                    else:
                        pe.wait_ge(acts_lo, it["acts"])
                        for g in range(4):
                            e = it["e"] + g
                            if g < 2:
                                pe.wait_ge(prod_read, e - 1)
                            else:
                                pe.wait_ge(mixed, it["mixed"] + 2 * (g - 1))
                            for half in range(2):
                                for n in range(2):
                                    a = (2 * g + n) * COLS + half * P
                                    mm = passes(prod[e % 2][:, half], lambda w, s, a=a: w[:, s, a:a + P],
                                                acts_h[:, 2 * g + n], acts_l[:, 2 * g + n], c % RING,
                                                n == 0, n == 1)
                            mm.then_inc(group_done if g < 3 else chunk_used, 1)
                    if late_statistics:
                        statistic(late_statistics.pop(0))
                elif kind == "stat":
                    if it["after_chunk"]:
                        late_statistics.append(it)
                    else:
                        statistic(it)
                elif kind == "tick":
                    tick(it)
                elif kind == "rope":
                    pe.wait_ge(prod_read, it["e"])
                    reader(pe, it["aux_reader"])
                    pe.matmul(aux[:], table("perm_" + it["which"]),
                              dests[it["dest"]][:, it["at"]:it["at"] + 2, :].rearrange("p a b -> p (a b)"),
                              start=True, stop=True).then_inc(aux_done, 1)
                elif kind == "head_norm":
                    pe.wait_ge(hn_squared, it["n"] + 1)
                    reader(pe, it["aux_reader"])
                    pe.matmul(aux[:], ones, hn_sq.rearrange("p a b -> p (a b)"), start=True,
                              stop=True).then_inc(aux_done, 1)

        @block.scalar
        def _(act):
            state = {"split": 0, "target": RING, "own": 0}

            def split(c, turn=0):
                if c >= N:
                    return
                act.wait_ge(raw_loaded[c % RAW], turn * (16 * 6 // RAW) + 16 * (c // RAW + 1))
                if c >= RING:
                    act.wait_ge(chunk_used, turn * 6 + c - RING + 1)
                act.copy(w_hi[:, c % RING], raw[:, c % RAW]).then_inc(hi_done, 1)

            def flush(upto=None):
                upto = state["target"] if upto is None else upto
                while state["split"] < min(upto, N):
                    split(state["split"])
                    state["split"] += 1

            def own(ins):
                ins.then_inc(act_step, 1)
                state["own"] += 1
                act.wait_ge(act_step, state["own"])

            def ffn_part(it, p, turn, split_too=True):
                kind, i = ffn_step(p)
                c = it["c"] + p
                m = it["m"] + i
                if kind == "up":
                    act.wait_ge(prod_read, turn * 4 + it["e"] + i + 1)
                    act.activation(four[:, 2, (m % 2) * S:(m % 2 + 1) * S], four[:, m % 2, 0:S],
                                   ACT.Silu).then_inc(silu_done, 1)
                if split_too:
                    split(c + RING, turn)
                if kind == "up":
                    act.wait_ge(mid_done, turn * 4 + m + 1)
                    act.copy(mix_h[:, i % 4], four[:, 3, (m % 2) * S:(m % 2 + 1) * S]).then_inc(mid_hi, 1)

            def squares(it, half, source, scale=None):
                if it["n"] and half == 0:
                    act.wait_ge(summed, 2 * it["n"])
                    act.wait_ge(mixed, it["mixed"])
                sl = slice(4 * half, 4 * half + 4)
                act.activation(sq[:, sl], source[:, sl], ACT.Square).then_inc(squared, 1)

            act.wait_ge(vecs_loaded, 16)
            for it in items:
                kind = it["kind"]
                if kind == "ffn":
                    flush()
                    assert state["split"] == it["c"] + RING
                    for p in range(5):
                        ffn_part(it, p, 0)
                    with act.Fori(0, 4, 1) as turn:
                        for p in range(5, 11):
                            ffn_part(it, p, turn)
                    for p in range(29, 33):
                        ffn_part(it, p, 0, split_too=(p < 31))
                    state["split"] = it["c"] + 31 + RING
                    state["target"] = it["c"] + 33 + RING
                elif kind in ("cols", "rows_out", "down", "group"):
                    flush()
                    if kind == "group":
                        for g in range(4):
                            if g < 3:
                                act.wait_ge(group_done, g + 1)
                            else:
                                act.wait_ge(chunk_used, it["c"] + 1)
                            for half in range(2):
                                act.activation(mix_h[:, 2 * g + half], prod[(it["e"] + g) % 2][:, half], ACT.Copy,
                                               scale=gain_col("pool_scale", 2 * g + half)).then_inc(mix_hi, 1)
                    state["target"] = it["c"] + 1 + RING
                elif kind == "prep":
                    if it["resid"] is not None:
                        flush(state["target"] - 1)
                    if it["src"] == "mem":
                        act.wait_ge(mem_loaded, it["mem_loaded"])
                    if it["acts_free"]:
                        act.wait_ge(chunk_used, it["acts_free"])
                    if it["first"]:
                        act.wait_ge(acts_lo, it["first"])
                    for kt in range(KT):
                        if it["src"] == "x":
                            if it["resid"] is not None:
                                act.wait_ge(x_new, it["x_new"] + kt // 2 + 1)
                            elif it["x_new"]:
                                act.wait_ge(x_new, it["x_new"])
                            else:
                                act.wait_ge(x_loaded[kt // 4], 16)
                            if it.get("double") and kt == 0:
                                act.wait_ge(dve_step, it["own"])
                        act.activation(acts_h[:, kt], sources[it["src"]][:, kt], ACT.Copy,
                                       scale=gain_col(it["gain"], kt)).then_inc(acts_hi, 1)
                        if kt % 4 == 3 and it["squares"]:
                            squares(it, kt // 4, sources[it["src"]])
                elif kind == "late_squares":
                    for half in range(2):
                        squares(it, half, sources[it["src"]])
                elif kind == "post_norm_sums":
                    act.wait_ge(summed, 2 * it["n"])
                    act.wait_ge(mixed, it["mixed"])
                    for half in range(2):
                        for b in (2 * half, 2 * half + 1):
                            act.wait_ge(y_copied, it["y_copied"] + b + 1)
                            ins = act.activation(sq[:, 2 * b:2 * b + 2], acc[b][:], ACT.Square)
                        ins.then_inc(squared, 1)
                elif kind == "final_squares":
                    for half in range(2):
                        if half == 0:
                            act.wait_ge(summed, 2 * it["n"])
                        for kt in range(4 * half, 4 * half + 4):
                            ins = act.activation(sq[:, kt], x[:, kt], ACT.Square, scale=gain_col("final_norm_g", kt))
                        ins.then_inc(squared, 1)
                elif kind == "stat":
                    flush()
                    if it["n"] == 0:
                        act.wait_ge(tabs_loaded, 16)
                    slot = 1 if it["src"] == "y" or it["final"] else 0
                    if it["src"] == "z":
                        act.wait_ge(scaled_ms, 1)
                        act.activation(rstd[:, 0], rstd[:, 0], ACT.Sqrt, bias=eps_col[0]).then_inc(rooted, 1)
                    else:
                        act.wait_ge(aux_done, it["aux"] + 1)
                        act.activation(rstd[:, slot], aux[:, 0:S + 2], ACT.Sqrt, bias=eps_col[0],
                                       scale=1.0 / D).then_inc(rooted, 1)
                elif kind == "tick":
                    if it["T"] and it["T"][0]["table"] != "decay":
                        unit, j = it["T"]
                        act.wait_ge(turned, unit["t"])
                        bank, dst = turned_at(unit), pt_slots[unit["u"] % 2]
                        if unit["shape"] is FULL:
                            act.copy(dst, bank).then_inc(turned_read, 1)
                        else:
                            act.copy(dst[:, 0:S], bank[:, 0:S])
                            act.copy(dst[:, S + P:2 * S], bank[:, S + P:2 * S]).then_inc(turned_read, 1)
                    if it["S"] and it["S"][0]["table"] != "decay":
                        unit, comp, j = it["S"]
                        act.wait_ge(max_done, unit["max_n"][comp])
                        full = unit["shape"] is FULL
                        src = score_at(j) if full else masked[:, j % 2, :]
                        for t, (at, width) in enumerate(unit["shape"]):
                            ins = act.activation(p_slots[j % 3][:, at:at + width], src[:, at:at + width], ACT.Exp,
                                                 bias=small[:, j % 3, 2 + t:3 + t], scale=unit["scale"],
                                                 accum_out=small[:, j % 3, 4 + t:5 + t])
                        ins.then_inc(exp_done, 1)
                    if it["V"]:
                        unit, j = it["V"]
                        act.wait_ge(o_done, unit["u"] + 1)
                        r0, r1 = unit["out_row"], unit["out_row"] + unit["v_width"]
                        if unit["out"] == "obuf":
                            act.wait_ge(acts_lo, it["acts_lo"])
                            act.copy(obuf[:, unit["tile"]], o_bank[:, 0]).then_inc(o_copied, 1)
                        else:
                            n = unit["out_tiles"]
                            act.copy(mix_h[r0:r1, unit["tile"]:unit["tile"] + n], o_bank[r0:r1, 0:n]
                                     ).then_inc(o_hi, 1)
                elif kind == "pool_split":
                    act.wait_ge(chunk_used, it["acts_free"])
                    act.wait_ge(acts_lo, it["first"])
                    for kt in (6, 7, 4, 5, 2, 3, 0, 1):
                        act.wait_ge(pooled, 4 - kt // 2)
                        act.copy(acts_h[:, kt], ybuf[:, kt]).then_inc(acts_hi, 1)
                elif kind == "head_squares":
                    pair = it["pair"]
                    act.wait_ge(o_copied, it["o_copied"])
                    act.wait_ge(mixed, it["mixed"])
                    act.wait_ge(summed, it["summed"])
                    act.activation(hn_sq, obuf[:, 2 * pair:2 * pair + 2], ACT.Square).then_inc(hn_squared, 1)
                elif kind == "head_norm":
                    pair = it["pair"]
                    act.wait_ge(aux_done, it["aux"] + 1)
                    act.activation(hn_root.rearrange("p a b -> p (a b)"), aux[:], ACT.Sqrt,
                                   bias=eps_col[1 if it["which"] == "diff" else 0],
                                   scale=1.0 / P).then_inc(hn_rooted, 1)
                elif kind == "head_split":
                    pair = it["pair"]
                    for n in range(2):
                        act.wait_ge(hn_scaled, it["n"] + 1)
                        act.copy(mix_h[:, HN_TILE[it["which"]] + 2 * pair + n], hn_on[:, n]).then_inc(mix_hi, 1)
                elif kind == "gate_silu":
                    act.wait_ge(prod_read, it["e"])
                    act.activation(xq[:, it["at"]:it["at"] + 2], xq[:, it["at"]:it["at"] + 2],
                                   ACT.Silu).then_inc(gated, 1)
                elif kind == "lambda":
                    act.wait_ge(lam_part, 1)
                    act.activation(lam[:, 2:4], lam[:, 0:2], ACT.Exp).then_inc(lam_part, 1)

        @block.vector
        def _(dve):
            state = {"split": 0, "target": RING, "own": 0}

            def split(c, turn=0):
                if c >= N:
                    return
                dve.wait_ge(hi_done, turn * 6 + c + 1)
                dve.tensor_tensor(w_lo[:, c % RING], raw[:, c % RAW], w_hi[:, c % RING].bitcast(F32),
                                  ALU.subtract).then_inc(lo_done, 1)

            def flush(upto=None):
                upto = state["target"] if upto is None else upto
                while state["split"] < min(upto, N):
                    split(state["split"])
                    state["split"] += 1

            def own(ins):
                ins.then_inc(dve_step, 1)
                state["own"] += 1
                dve.wait_ge(dve_step, state["own"])

            def mid_low(it, i, turn):
                m = it["m"] + i
                dve.wait_ge(mid_hi, turn * 4 + m + 1)
                dve.tensor_tensor(mix_l[:, i % 4], four[:, 3, (m % 2) * S:(m % 2 + 1) * S],
                                  mix_h[:, i % 4].bitcast(F32), ALU.subtract).then_inc(mid_lo, 1)

            def ffn_part(it, p, turn, split_too=True):
                kind, i = ffn_step(p)
                c = it["c"] + p
                if kind == "up":
                    m = it["m"] + i
                    e = it["e"] + i
                    dve.wait_ge(chunk_used, turn * 6 + c + 1)
                    dve.tensor_tensor(four[:, m % 2, :].rearrange("p (a b) -> p a b", a=2), prod[e % 2][:],
                                      bcast(rstd[:, 0, 0:S], 2), ALU.mult).then_inc(prod_read, 1)
                    if i % 2:
                        mid_low(it, i - 1, turn)
                elif p < 32:
                    mid_low(it, 2 * i + 3, turn)
                if split_too:
                    split(c + RING - 1, turn)
                if kind == "up":
                    dve.wait_ge(silu_done, turn * 4 + m + 1)
                    dve.tensor_tensor(four[:, 3, (m % 2) * S:(m % 2 + 1) * S],
                                      four[:, 2, (m % 2) * S:(m % 2 + 1) * S], four[:, m % 2, S:2 * S],
                                      ALU.mult).then_inc(mid_done, 1)

            def sum_half(n, half):
                dve.wait_ge(squared, 2 * n + half + 1)
                if n and half == 0:
                    dve.wait_ge(aux_done, state["aux"])
                dve.tensor_reduce(sums[:, half], sq[:, 4 * half:4 * half + 4].rearrange("p k t -> p t k"), AX.X,
                                  ALU.add).then_inc(summed, 1)

            def lo_tile(it, kt):
                dve.wait_ge(acts_hi, it["first"] + kt + 1)
                dve.scalar_tensor_tensor(out=acts_l[:, kt], in0=sources[it["src"]][:, kt],
                                         scalar=gain_col(it["gain"], kt), in1=acts_h[:, kt].bitcast(F32),
                                         op0=ALU.mult, op1=ALU.subtract).then_inc(acts_lo, 1)

            def wait_sum(it, b):
                if b < 3:
                    dve.wait_ge(acc_done, it["y"] - 3 + b + 1)
                else:
                    dve.wait_ge(chunk_used, it["y_chunk"])

            def add_pair(it, b, scale):
                wait_sum(it, b)
                dve.scalar_tensor_tensor(out=x[:, 2 * b:2 * b + 2], in0=acc[b][:], scalar=scale,
                                               in1=x[:, 2 * b:2 * b + 2], op0=ALU.mult, op1=ALU.add
                                         ).then_inc(x_new, 1)

            def post_pair(it, b):
                own(dve.tensor_tensor(ybuf[:, 2 * b:2 * b + 2], ybuf[:, 2 * b:2 * b + 2],
                                      bcast(rstd[:, 1, 0:S], 2), ALU.mult))
                dve.tensor_tensor(x[:, 2 * b:2 * b + 2], x[:, 2 * b:2 * b + 2], ybuf[:, 2 * b:2 * b + 2],
                                  ALU.add).then_inc(x_new, 1)

            def weights(it):
                unit, comp, j = it["F"]
                p = p_slots[j % 3]
                last = comp == unit["comps"] - 1
                if unit["table"] == "decay":
                    dve.wait_ge(score_done, j + 1)
                    dve.wait_ge(o_done, unit["u"] - 2)
                    d = table("decay")[:, unit["head"] * S:(unit["head"] + 1) * S]
                    dve.tensor_tensor(p[:, 0:S], score[j % 2][:, 0:S], d, ALU.mult)
                    dve.tensor_tensor(p[:, S:S + P], score[j % 2][:, S:S + P], d[:, 0:P],
                                      ALU.mult).then_inc(decayed, 1)
                else:
                    dve.wait_ge(exp_done, unit["max_n"][comp])
                    own(dve.reciprocal(small[:, j % 3, 6:8], small[:, j % 3, 4:6]))
                    if comp == 0:
                        for t, (at, width) in enumerate(unit["shape"]):
                            ins = dve.tensor_scalar(p[:, at:at + width], p[:, at:at + width],
                                                    small[:, j % 3, 6 + t:7 + t], None, ALU.mult)
                        if last:
                            ins.then_inc(weights_done, 1)
                        else:
                            own(ins)
                    else:
                        own(dve.tensor_scalar(small[:, j % 3, 6:8], small[:, j % 3, 6:8], lam[:, 8:9], None,
                                              ALU.mult))
                        for t, (at, width) in enumerate(unit["shape"]):
                            ins = dve.scalar_tensor_tensor(
                                out=p[:, at:at + width], in0=p[:, at:at + width],
                                scalar=small[:, j % 3, 6 + t:7 + t], in1=p_slots[(j - 1) % 3][:, at:at + width],
                                op0=ALU.mult, op1=ALU.add)
                        ins.then_inc(weights_done, 1)

            def tick(it):
                if it["S"] and it["S"][0]["table"] != "decay":
                    unit, comp, j = it["S"]
                    dve.wait_ge(score_done, j + 1)
                    src = score_at(j)
                    if unit["shape"] is not FULL:
                        slope = 1.0 if unit["slope"] is None else unit["slope"] / unit["scale"]
                        own(dve.scalar_tensor_tensor(out=masked[:, j % 2, :], in0=table(unit["table"]), scalar=slope,
                                                     in1=src[:, 0:384], op0=ALU.mult, op1=ALU.add))
                        src = masked[:, j % 2, :]
                    for t, (at, width) in enumerate(unit["shape"]):
                        ins = dve.tensor_reduce(small[:, j % 3, t:t + 1], src[:, at:at + width], AX.X, ALU.max,
                                                negate=True)
                    own(ins)
                    dve.tensor_scalar(small[:, j % 3, 2:4], small[:, j % 3, 0:2], unit["scale"], None,
                                      ALU.mult).then_inc(max_done, 1)
                if it["V"] and it["V"][0]["out"] == "mix":
                    unit, j = it["V"]
                    dve.wait_ge(o_hi, unit["o_hi"])
                    r0, r1 = unit["out_row"], unit["out_row"] + unit["v_width"]
                    for n in range(unit["out_tiles"]):
                        ins = dve.tensor_tensor(mix_l[r0:r1, unit["tile"] + n], o_bank[r0:r1, n],
                                                mix_h[r0:r1, unit["tile"] + n].bitcast(F32), ALU.subtract)
                        ins.then_inc(mixed, 1)

            dve.wait_ge(vecs_loaded, 16)
            own(dve.tensor_tensor(both_g[:], vecs[:, GAIN["final_norm_g"]:GAIN["final_norm_g"] + KT],
                                  vecs[:, GAIN["g_pre_mix"]:GAIN["g_pre_mix"] + KT], ALU.mult))
            for it in items:
                kind = it["kind"]
                if kind == "ffn":
                    flush()
                    assert state["split"] == it["c"] + RING
                    for p in range(5):
                        ffn_part(it, p, 0, split_too=(p > 0))
                        if p == 1:
                            mid_low(it, 1, 0)
                    with dve.Fori(0, 4, 1) as turn:
                        for p in range(5, 11):
                            ffn_part(it, p, turn)
                    for p in range(29, 33):
                        ffn_part(it, p, 0, split_too=(p < 32))
                    state["split"] = it["c"] + 31 + RING
                    state["target"] = it["c"] + 33 + RING
                elif kind in ("cols", "rows_out", "down", "group"):
                    flush()
                    c = it["c"]
                    if kind == "cols":
                        e = it["e"]
                        dve.wait_ge(chunk_used, c + 1)
                        if it["dest"] == "u":
                            out = padded[:, it["at"]:it["at"] + 2, PAD:PAD + S]
                        else:
                            out = dests[it["dest"]][:, it["at"]:it["at"] + 2]
                        dve.tensor_tensor(out, prod[e % 2][:], bcast(rstd[:, 0, 0:S], 2),
                                          ALU.mult).then_inc(prod_read, 1)
                    elif kind == "rows_out":
                        e = it["e"]
                        dve.wait_ge(chunk_used, c + 1)
                        for t in range(2):
                            ins = dve.tensor_scalar(tok_dests[it["dest"]][:, t, it["at"]:it["at"] + COLS],
                                                    prod[e % 2][:, t], rstd[:, 0, S + t:S + t + 1], None, ALU.mult)
                        ins.then_inc(prod_read, 1)
                    elif kind == "group":
                        for g in range(4):
                            for half in range(2):
                                tile = 2 * g + half
                                dve.wait_ge(mix_hi, it["mix_hi"] + 2 * g + 2)
                                dve.scalar_tensor_tensor(
                                    out=mix_l[:, tile], in0=prod[(it["e"] + g) % 2][:, half],
                                    scalar=gain_col("pool_scale", tile), in1=mix_h[:, tile].bitcast(F32),
                                    op0=ALU.mult, op1=ALU.subtract).then_inc(mixed, 1)
                    state["target"] = c + 1 + RING
                elif kind == "prep":
                    if it["resid"] is not None:
                        flush(state["target"] - 1)
                        for b in range(4):
                            if it["resid"] == "post":
                                post_pair(it, b)
                            else:
                                add_pair(it, b, it["resid"])
                            if b:
                                lo_tile(it, 2 * b - 2)
                                lo_tile(it, 2 * b - 1)
                        sum_half(it["n"], 0)
                        lo_tile(it, 6)
                        lo_tile(it, 7)
                    else:
                        for kt in range(KT):
                            lo_tile(it, kt)
                            if kt == 5 and it["squares"]:
                                sum_half(it["n"], 0)
                    if it["squares"]:
                        sum_half(it["n"], 1)
                elif kind == "residual":
                    for b in range(4):
                        add_pair(it, b, it["scale"])
                elif kind == "post_norm_sums":
                    for b in range(4):
                        wait_sum(it, b)
                        for half in range(2):
                            ins = dve.tensor_scalar(ybuf[:, 2 * b + half], acc[b][:, half],
                                                    gain_col(it["gain"], 2 * b + half), None, ALU.mult)
                        ins.then_inc(y_copied, 1)
                    for half in range(2):
                        sum_half(it["n"], half)
                elif kind in ("final_squares", "late_squares"):
                    for half in range(2):
                        sum_half(it["n"], half)
                elif kind == "stat":
                    flush()
                    state["aux"] = it["aux"] + 1
                    if it["src"] == "z":
                        dve.wait_ge(aux_done, it["aux"] + 1)
                        own(dve.scalar_tensor_tensor(out=rstd[:, 0], in0=aux[:, 0:S + 2], scalar=1.0 / D,
                                                     in1=rstd[:, 1], op0=ALU.mult, op1=ALU.mult))
                        dve.tensor_tensor(rstd[:, 0], rstd[:, 0], rstd[:, 1], ALU.mult).then_inc(scaled_ms, 1)
                        dve.wait_ge(rooted, it["n"] + 1)
                        own(dve.reciprocal(rstd[:, 0], rstd[:, 0]))
                        own(dve.tensor_tensor(rstd[:, 0], rstd[:, 0], rstd[:, 1], ALU.mult))
                    else:
                        slot = 1 if it["src"] == "y" or it["final"] else 0
                        dve.wait_ge(rooted, it["n"] + 1)
                        own(dve.reciprocal(rstd[:, slot], rstd[:, slot]))
                elif kind == "x_final":
                    for kt in range(KT):
                        ins = dve.scalar_tensor_tensor(out=x[:, kt], in0=x[:, kt], scalar=gain_col("final_norm_g", kt),
                                                       in1=rstd[:, 1, 0:S], op0=ALU.mult, op1=ALU.mult)
                        if kt % 2:
                            ins.then_inc(x_new, 1)
                elif kind == "post_norm":
                    for b in range(4):
                        post_pair(it, b)
                elif kind == "lambda":
                    dve.wait_ge(lam_loaded, 16)
                    own(dve.tensor_tensor(lam_prod, lamb[:, :, 0], lamb[:, :, 1], ALU.mult))
                    dve.tensor_reduce(lam[:, 0:2], lam_prod, AX.X, ALU.add).then_inc(lam_part, 1)
                    dve.wait_ge(lam_part, 2)
                    own(dve.tensor_tensor(lam[:, 4:5], lam[:, 3:4], lam[:, 2:3], ALU.subtract))
                    own(dve.tensor_scalar(lam[:, 8:9], lam[:, 4:5], -LAM_INIT, None, ALU.add))
                    own(dve.tensor_scalar(lam[:, 9:10], vecs[:, DIFF_G:DIFF_G + 1], 1.0 - LAM_INIT, None,
                                          ALU.mult))
                elif kind == "tick":
                    tick(it)
                elif kind == "weights":
                    weights(it)
                elif kind == "rope":
                    dve.wait_ge(aux_done, it["aux"] + 1)
                    t = dests[it["dest"]][:, it["at"]:it["at"] + 2]
                    rot = rotated
                    own(dve.tensor_tensor(rot, aux[:].rearrange("p (a b) -> p a b", a=2),
                                          bcast(table("sin_" + it["which"]), 2), ALU.mult))
                    own(dve.tensor_tensor(t, t, bcast(table("cos_" + it["which"]), 2), ALU.mult))
                    dve.tensor_tensor(t, t, rot, ALU.add).then_inc(roped, 1)
                elif kind == "pool":
                    g = it["g"]
                    if g == 3:
                        for buf in shifted:
                            dve.memset(buf[:, :, 0:PAD], 0.0)
                        own(dve.memset(padded[:, :, 0:PAD], 0.0))
                    else:
                        dve.wait_ge(pooled, 3 - g)
                    dve.wait_ge(prod_read, it["e"])
                    u = padded[:, 2 * g:2 * g + 2]
                    src = u
                    for n in range(g + 1):
                        dst = shifted[n % 2]
                        own(dve.tensor_tensor(dst[:, :, PAD:], src[:, :, PAD:],
                                              src[:, :, PAD - (1 << n):PAD + S - (1 << n)], ALU.add))
                        src = dst
                    w = POOL_WINDOWS[g]
                    out = ybuf[:, 2 * g:2 * g + 2]
                    dve.scalar_tensor_tensor(out=out, in0=src[:, :, PAD:], scalar=1.0 / w, in1=u[:, :, PAD:],
                                             op0=ALU.mult, op1=ALU.subtract)
                    other = shifted[(g + 1) % 2]
                    own(dve.tensor_tensor(other[:, :, PAD:2 * PAD], src[:, :, PAD:2 * PAD],
                                          table("inv_count")[:, 16 * g:16 * g + 16].unsqueeze(1).broadcast_to(
                                              [P, 2, 16]), ALU.mult))
                    dve.tensor_tensor(out[:, :, 0:16], other[:, :, PAD:2 * PAD], u[:, :, PAD:2 * PAD],
                                      ALU.subtract).then_inc(pooled, 1)
                elif kind == "pool_split":
                    for n, kt in enumerate((6, 7, 4, 5, 2, 3, 0, 1)):
                        dve.wait_ge(acts_hi, it["first"] + n + 1)
                        dve.tensor_tensor(acts_l[:, kt], ybuf[:, kt], acts_h[:, kt].bitcast(F32),
                                          ALU.subtract).then_inc(acts_lo, 1)
                elif kind == "head_norm":
                    pair = it["pair"]
                    dve.wait_ge(hn_rooted, it["n"] + 1)
                    r = hn_root
                    own(dve.reciprocal(r, r))
                    src = obuf[:, 2 * pair:2 * pair + 2]
                    if it["which"] == "diff":
                        dve.scalar_tensor_tensor(out=hn_on, in0=src, scalar=lam[:, 9:10], in1=r, op0=ALU.mult,
                                                 op1=ALU.mult).then_inc(hn_scaled, 1)
                    else:
                        own(dve.tensor_tensor(hn_on, src, r, ALU.mult))
                        dve.wait_ge(gated, pair + 1)
                        dve.tensor_tensor(hn_on, hn_on, xq[:, 2 * pair:2 * pair + 2], ALU.mult
                                              ).then_inc(hn_scaled, 1)
                elif kind == "head_split":
                    pair = it["pair"]
                    for n in range(2):
                        tile = HN_TILE[it["which"]] + 2 * pair + n
                        dve.wait_ge(mix_hi, it["mix_hi"] + n + 1)
                        dve.tensor_tensor(mix_l[:, tile], hn_on[:, n], mix_h[:, tile].bitcast(F32),
                                          ALU.subtract).then_inc(mixed, 1)


def number(plan):
    plan.score_reader, plan.o_reader = {}, {}
    aux_reader = None
    pending_double = False
    late_readers = []
    n = dict(acc_turned=0, acts=0, decay=0, o_copied=0, rope=0, max=0, turned=0, o_hi=0, mix_hi=0, mixed=0, hn=0, stats=0, y_copied=0, mem=0)
    for it in plan.items:
        kind = it["kind"]
        if kind == "tick":
            if it["S"]:
                unit, comp, j = it["S"]
                if unit["table"] != "decay":
                    n["max"] += 1
                    unit.setdefault("max_n", {})[comp] = n["max"]
                    plan.score_reader[j] = ("exp_done", n["max"])
                else:
                    n["decay"] += 1
                    unit["d"] = n["decay"]
                    plan.score_reader[j] = ("decayed", n["decay"])
                if j in plan.late_steps:
                    late_readers = late_readers[-1:] + [plan.score_reader[j]]
            if it["T"] and it["T"][0]["table"] != "decay":
                n["turned"] += 1
                it["T"][0]["t"] = n["turned"]
                if it["T"][0]["late"]:
                    it["aux_reader"], aux_reader = aux_reader, ("turned_read", n["turned"])
                else:
                    n["acc_turned"] = n["turned"]
            if it["V"]:
                unit = it["V"][0]
                if unit["out"] == "mix":
                    n["o_hi"] += 1
                    unit["o_hi"] = n["o_hi"]
                    n["mixed"] += unit["out_tiles"]
                    plan.o_reader[unit["u"]] = ("mixed", n["mixed"])
                else:
                    it["acts_lo"] = n["acts"]
                    n["o_copied"] += 1
                    plan.o_reader[unit["u"]] = ("o_copied", n["o_copied"])
        elif kind == "stat":
            it["final"] = pending_double
            pending_double = False
            n["stats"] += 1
            if it["src"] == "z":
                it["aux_reader"], aux_reader = aux_reader, ("rooted", n["stats"])
                continue
            it["aux_reader"], aux_reader = aux_reader, ("rooted", n["stats"])
        elif kind == "rope":
            n["rope"] += 1
            it["aux_reader"], aux_reader = aux_reader, ("roped", n["rope"])
        elif kind in ("post_norm_sums", "late_squares"):
            it["mixed"] = n["mixed"]
        elif kind == "prep":
            it["mixed"] = n["mixed"]
            it["own"] = 1
            pending_double = it.get("double", False)
            n["acts"] += KT
            if it["src"] == "mem":
                n["mem"] += 1
                it["mem_loaded"] = 16 if n["mem"] < 3 else 32
        elif kind == "pool_split":
            n["acts"] += KT
        elif kind == "head_squares":
            it["o_copied"], it["mixed"], it["summed"] = n["o_copied"], n["mixed"], 2 * n["stats"]
        elif kind == "group":
            it["mix_hi"], it["mixed"] = n["mix_hi"], n["mixed"]
            n["mix_hi"] += 8
            n["mixed"] += 8
        elif kind == "head_split":
            it["mix_hi"] = n["mix_hi"]
            n["mix_hi"] += 2
            n["mixed"] += 2
        elif kind == "head_norm":
            n["hn"] += 1
            it["aux_reader"], aux_reader = aux_reader, ("hn_rooted", n["hn"])
        elif kind == "load_mem2":
            it["mixed"] = n["mixed"]
        if kind in ("down", "ffn"):
            it["t"] = n["acc_turned"]
        it["late_readers"] = []
        if kind in ("cols", "rows_out", "group", "ffn"):
            it["late_readers"], late_readers = late_readers, []
    assert n["mixed"] == plan.mixed


def kernel(**inputs):
    import concourse.bacc as bacc
    from concourse.bass_utils import run_bass_kernel_spmd

    inputs = {k: np.asarray(v) for k, v in inputs.items()}
    plan = make_plan()
    number(plan)
    weights = np.empty((plan.c, P, CHUNK), np.float32)
    for n, source in enumerate(plan.chunks):
        lay_out_chunk(inputs, source, weights[n])
    g = inputs["norm_g"]
    gains = {f"norm_g{i}{j}": g[i, j] for i in range(2) for j in range(3)}
    gains.update(mem_norm_g=inputs["mem_norm_g"], pool_scale=inputs["pool_scale"][0],
                 final_norm_g=inputs["final_norm_g"])
    for name in GAINS[9:]:
        gains[name] = inputs[name + "_2"][0]
    vecs = np.concatenate([columns(gains[name]) for name in GAINS] + [columns(inputs["diff_norm_g"][0])], 1)
    lam = np.ascontiguousarray(np.broadcast_to(inputs["diff_lambda"].reshape(1, 2, 2, 64), (P, 2, 2, 64)))
    arrays = {"x": features_first(inputs["x"]), "mem": features_first(inputs["mem"]),
              "mem2": features_first(inputs["mem_2"]), "weights": weights, "vecs": np.ascontiguousarray(vecs),
              "tabs": tables(), "lambda": lam}
    nc = bacc.Bacc("TRN2", target_bir_lowering=False, num_devices=1)
    A = {k: nc.dram_tensor(f"in_{k}_dram", a.shape, F32, kind="ExternalInput").ap() for k, a in arrays.items()}
    A["out"] = nc.dram_tensor("out_dram", (P, KT, S), F32, kind="ExternalOutput").ap()
    build(nc, A, plan)
    r = run_bass_kernel_spmd(nc, [{f"in_{k}_dram": a for k, a in arrays.items()}], core_ids=[0])
    out = r.results[0]["out_dram"]
    return np.ascontiguousarray(out.transpose(1, 0, 2).reshape(D, S).T)[None]
```
